# Optimizing a Trainium2 kernel written in Bass

```python
import jax, jax.numpy as jnp
from jax import lax
import numpy as np
import math

D_MODEL = 1024
BATCH = 1
SEQ = 1024
DEPTH = 1

CHUNK = 64
N_BRANCH = 3
BRANCH_WIDTH = D_MODEL // 2
POOL_WINDOWS = (2, 4, 8, 16)
N_POOL_GROUPS = len(POOL_WINDOWS)
POOL_GROUP = BRANCH_WIDTH // N_POOL_GROUPS
CONV_K = 3
SB_HEAD_DIM = 64
SB_HEADS = BRANCH_WIDTH // SB_HEAD_DIM
Q_BLOCK = 128
RMS_EPS = 1e-6
IN_SIZES = (BRANCH_WIDTH,) * 10 + (N_BRANCH * D_MODEL,)
N_IN = sum(IN_SIZES)


def _split_points():
    return [int(p) for p in np.cumsum(IN_SIZES)[:-1]]

def rms_norm(x, g):
    xf = x.astype(jnp.float32)
    y = xf * lax.rsqrt(jnp.mean(xf * xf, axis=-1, keepdims=True) + RMS_EPS)
    return (y * g.astype(jnp.float32)).astype(x.dtype)

def pool_mixer(v, w_group, scale):
    b, s, _ = v.shape
    vg = v.astype(jnp.float32).reshape(b, s, N_POOL_GROUPS, POOL_GROUP)
    csum = jnp.cumsum(vg, axis=1)
    pos = jnp.arange(s)
    outs = []
    for gi, w in enumerate(POOL_WINDOWS):
        c = csum[:, :, gi]
        lag = jnp.pad(c[:, :s - w], ((0, 0), (w, 0), (0, 0)))
        cnt = jnp.minimum(pos + 1, w).astype(jnp.float32)[None, :, None]
        outs.append((c - lag) / cnt - vg[:, :, gi])
    pooled = jnp.stack(outs, axis=2).astype(v.dtype)
    mixed = jnp.einsum('bsgc,gcd->bsgd', pooled, w_group)
    return mixed.reshape(b, s, BRANCH_WIDTH) * scale

def conv_mixer(xc, gate_b, gate_c, w, bias):
    z = gate_c * xc
    y = lax.conv_general_dilated(
        z, w[:, None, :].astype(z.dtype), window_strides=(1,), padding=[(CONV_K - 1, 0)],
        dimension_numbers=('NWC', 'WIO', 'NWC'), feature_group_count=BRANCH_WIDTH)
    return gate_b * (y + bias)

def stick_breaking_attention(q, k, v):
    b, s, _ = q.shape
    nblk = s // Q_BLOCK
    qb = q.reshape(b, nblk, Q_BLOCK, SB_HEADS, SB_HEAD_DIM).transpose(1, 0, 2, 3, 4)
    kf = k.reshape(b, s, SB_HEADS, SB_HEAD_DIM).astype(jnp.float32)
    vf = v.reshape(b, s, SB_HEADS, SB_HEAD_DIM).astype(jnp.float32)
    key_pos = jnp.arange(s)
    scale = SB_HEAD_DIM ** -0.5

    def block(args):
        qi, i = args
        logits = jnp.einsum('bqhd,bkhd->bhqk', qi.astype(jnp.float32), kf) * scale
        q_pos = i * Q_BLOCK + jnp.arange(Q_BLOCK)
        mask = key_pos[None, :] < q_pos[:, None]
        log_keep = jnp.where(mask, jax.nn.log_sigmoid(-logits), 0.0)
        later = lax.cumsum(log_keep, axis=3, reverse=True) - log_keep
        weights = jnp.where(mask, jnp.exp(jax.nn.log_sigmoid(logits) + later), 0.0)
        return jnp.einsum('bhqk,bkhd->bqhd', weights, vf)

    out = lax.map(block, (qb, jnp.arange(nblk)))
    return out.transpose(1, 0, 2, 3, 4).reshape(b, s, BRANCH_WIDTH).astype(q.dtype)

def hybrid_layer(x, g_pre, w_in, pool_w, pool_scale, conv_w, conv_b, w_branch, w_out, g_post):
    b, s, _ = x.shape
    h = rms_norm(x, g_pre)
    u = jnp.einsum('bsd,dn->bsn', h, w_in)
    (pool_v, pool_g, conv_x, conv_gb, conv_gc, conv_g,
     sb_q, sb_k, sb_v, sb_g, merge) = jnp.split(u, _split_points(), axis=-1)
    y_pool = pool_mixer(pool_v, pool_w, pool_scale) * jax.nn.silu(pool_g)
    y_conv = conv_mixer(conv_x, conv_gb, conv_gc, conv_w, conv_b) * jax.nn.silu(conv_g)
    y_sb = stick_breaking_attention(sb_q, sb_k, sb_v) * jax.nn.silu(sb_g)
    branches = jnp.stack([y_pool, y_conv, y_sb], axis=2)
    proj = jnp.einsum('bsnw,nwd->bsnd', branches, w_branch)
    gates = jax.nn.sigmoid(merge.reshape(b, s, N_BRANCH, D_MODEL))
    merged = jnp.sum(gates * proj, axis=2)
    out = jnp.einsum('bsd,de->bse', merged, w_out)
    return x + rms_norm(out, g_post)

def first_inputs(seed: int = 0) -> dict:
    key = jax.random.key(seed)
    ks = jax.random.split(key, 10)
    f32 = jnp.float32
    x = jax.random.normal(ks[0], (BATCH, SEQ, D_MODEL), f32)
    pre_norm_g = 1.0 + 0.05 * jax.random.normal(ks[1], (DEPTH, D_MODEL), f32)
    w_in = jax.random.normal(ks[2], (DEPTH, D_MODEL, N_IN), f32) * D_MODEL ** -0.5
    pool_w = jax.random.normal(ks[3], (DEPTH, N_POOL_GROUPS, POOL_GROUP, POOL_GROUP), f32) * POOL_GROUP ** -0.5
    pool_scale = 1.0 + 0.1 * jax.random.normal(ks[4], (DEPTH, BRANCH_WIDTH), f32)
    conv_w = jax.random.normal(ks[5], (DEPTH, CONV_K, BRANCH_WIDTH), f32) * CONV_K ** -0.5
    conv_b = 0.01 * jax.random.normal(ks[6], (DEPTH, BRANCH_WIDTH), f32)
    w_branch = jax.random.normal(ks[7], (DEPTH, N_BRANCH, BRANCH_WIDTH, D_MODEL), f32) * BRANCH_WIDTH ** -0.5
    w_out = jax.random.normal(ks[8], (DEPTH, D_MODEL, D_MODEL), f32) * D_MODEL ** -0.5
    post_norm_g = 1.0 + 0.05 * jax.random.normal(ks[9], (DEPTH, D_MODEL), f32)
    return {"x": x, "pre_norm_g": pre_norm_g, "w_in": w_in, "pool_w": pool_w,
            "pool_scale": pool_scale, "conv_w": conv_w, "conv_b": conv_b,
            "w_branch": w_branch, "w_out": w_out, "post_norm_g": post_norm_g}

def first_block(x, pre_norm_g, w_in, pool_w, pool_scale, conv_w, conv_b, w_branch, w_out, post_norm_g):
    for l in range(DEPTH):
        x = hybrid_layer(x, pre_norm_g[l], w_in[l], pool_w[l], pool_scale[l], conv_w[l],
                         conv_b[l], w_branch[l], w_out[l], post_norm_g[l])
    return x


EPS = 1e-6
D_MIX = D_MODEL
CONV_K_2 = 4

SSD_HEADS = 8
SSD_HEAD_DIM = 64
SSD_DIM = SSD_HEADS * SSD_HEAD_DIM
SSD_GROUPS = 2
SSD_STATE = 128
SSD_CONV_DIM = SSD_DIM + 2 * SSD_GROUPS * SSD_STATE

ATT_HEADS = 4
ATT_KV_HEADS = 2
ATT_HEAD_DIM = 64
ATT_DIM = ATT_HEADS * ATT_HEAD_DIM
ATT_KV_DIM = ATT_KV_HEADS * ATT_HEAD_DIM
WINDOW = 128
WIN_CHUNKS = WINDOW // CHUNK

GDN_HEADS = 4
GDN_HEAD_K = 64
GDN_HEAD_V = 64
GDN_KDIM = GDN_HEADS * GDN_HEAD_K
GDN_DIM = GDN_HEADS * GDN_HEAD_V
GDN_CONV_DIM = 2 * GDN_KDIM + GDN_DIM

FF = ((8 * D_MODEL // 3 + 255) // 256) * 256

IN_SIZES_2 = (ATT_DIM, ATT_KV_DIM, ATT_KV_DIM,
            SSD_DIM, SSD_CONV_DIM, SSD_HEADS,
            GDN_CONV_DIM, GDN_DIM, GDN_HEADS, GDN_HEADS)
IN_COLS = sum(IN_SIZES_2)


def _offsets(sizes):
    out, acc = [], 0
    for s in sizes[:-1]:
        acc += s
        out.append(acc)
    return out

def rmsnorm(x, w):
    xf = x.astype(jnp.float32)
    y = xf * lax.rsqrt(jnp.mean(xf * xf, axis=-1, keepdims=True) + EPS)
    return (y * w.astype(jnp.float32)).astype(x.dtype)

def l2norm(x):
    return x * lax.rsqrt(jnp.sum(x * x, axis=-1, keepdims=True) + EPS)

def causal_dwconv(x, w, b=None):
    k = w.shape[0]
    t = x.shape[1]
    xp = jnp.pad(x, ((0, 0), (k - 1, 0), (0, 0)))
    y = xp[:, 0:t] * w[0]
    for i in range(1, k):
        y = y + xp[:, i:i + t] * w[i]
    if b is not None:
        y = y + b
    return y

def alibi_slopes(n):
    return 2.0 ** (-8.0 * jnp.arange(1, n + 1, dtype=jnp.float32) / n)

def lower_exp_diff(cs):
    n = cs.shape[-1]
    tril = jnp.tril(jnp.ones((n, n), dtype=bool))
    diff = cs[..., :, None] - cs[..., None, :]
    return jnp.where(tril, jnp.exp(jnp.where(tril, diff, 0.0)), 0.0)

def swa_sink_alibi(q, k, v, sinks):
    bsz, t = q.shape[0], q.shape[1]
    nc = t // CHUNK
    grp = ATT_HEADS // ATT_KV_HEADS
    band = (WIN_CHUNKS + 1) * CHUNK
    qc = q.reshape(bsz, nc, CHUNK, ATT_KV_HEADS, grp, ATT_HEAD_DIM)
    padw = ((0, 0), (WIN_CHUNKS * CHUNK, 0), (0, 0))
    kp = jnp.pad(k, padw).reshape(bsz, nc + WIN_CHUNKS, CHUNK, ATT_KV_HEADS, ATT_HEAD_DIM)
    vp = jnp.pad(v, padw).reshape(bsz, nc + WIN_CHUNKS, CHUNK, ATT_KV_HEADS, ATT_HEAD_DIM)
    kb = jnp.concatenate([kp[:, j:j + nc] for j in range(WIN_CHUNKS + 1)], axis=2)
    vb = jnp.concatenate([vp[:, j:j + nc] for j in range(WIN_CHUNKS + 1)], axis=2)
    s = jnp.einsum('bcikgd,bcjkd->bckgij', qc, kb).astype(jnp.float32) * (ATT_HEAD_DIM ** -0.5)
    qi = jnp.arange(CHUNK)[:, None]
    kj = jnp.arange(band)[None, :]
    dist = jnp.abs(qi + WIN_CHUNKS * CHUNK - kj).astype(jnp.float32)
    slopes = alibi_slopes(ATT_HEADS).reshape(ATT_KV_HEADS, grp)
    s = s - slopes[:, :, None, None] * dist
    key_chunk = jnp.arange(nc)[:, None] - WIN_CHUNKS + (jnp.arange(band) // CHUNK)[None, :]
    valid = key_chunk >= 0
    s = jnp.where(valid[None, :, None, None, None, :], s, -jnp.inf)
    sink = jnp.broadcast_to(sinks.astype(jnp.float32).reshape(1, 1, ATT_KV_HEADS, grp, 1, 1),
                            s.shape[:-1] + (1,))
    p = jax.nn.softmax(jnp.concatenate([s, sink], axis=-1), axis=-1)[..., :band]
    o = jnp.einsum('bckgij,bcjkd->bcikgd', p.astype(v.dtype), vb)
    return o.reshape(bsz, t, ATT_DIM)

def ssd_mixer(z, xbc, dt, conv_w, conv_b, dt_bias, a_log, d_skip, norm_w):
    bsz, t = xbc.shape[0], xbc.shape[1]
    nc = t // CHUNK
    hpg = SSD_HEADS // SSD_GROUPS
    xbc = jax.nn.silu(causal_dwconv(xbc, conv_w, conv_b)).astype(jnp.float32)
    xs, bm, cm = jnp.split(xbc, [SSD_DIM, SSD_DIM + SSD_GROUPS * SSD_STATE], axis=-1)
    xs = xs.reshape(bsz, t, SSD_HEADS, SSD_HEAD_DIM)
    bm = jnp.repeat(bm.reshape(bsz, t, SSD_GROUPS, SSD_STATE), hpg, axis=2)
    cm = jnp.repeat(cm.reshape(bsz, t, SSD_GROUPS, SSD_STATE), hpg, axis=2)
    dt = jax.nn.softplus(dt.astype(jnp.float32) + dt_bias.astype(jnp.float32))
    a = -jnp.exp(a_log.astype(jnp.float32))
    xc = (xs * dt[..., None]).reshape(bsz, nc, CHUNK, SSD_HEADS, SSD_HEAD_DIM)
    bc = bm.reshape(bsz, nc, CHUNK, SSD_HEADS, SSD_STATE)
    cc = cm.reshape(bsz, nc, CHUNK, SSD_HEADS, SSD_STATE)
    da = (dt * a).reshape(bsz, nc, CHUNK, SSD_HEADS).transpose(0, 3, 1, 2)
    a_cs = jnp.cumsum(da, axis=-1)
    lmat = lower_exp_diff(a_cs)
    scores = jnp.einsum('bclhn,bcshn->bhcls', cc, bc) * lmat
    y_diag = jnp.einsum('bhcls,bcshp->bclhp', scores, xc)
    decay_states = jnp.exp(a_cs[..., -1:] - a_cs)
    chunk_states = jnp.einsum('bclhn,bhcl,bclhp->bchpn', bc, decay_states, xc)
    chunk_decay = jnp.exp(a_cs[..., -1])

    def step(state, inp):
        new, dec = inp
        return state * dec[..., None, None] + new, state

    init = jnp.zeros((bsz, SSD_HEADS, SSD_HEAD_DIM, SSD_STATE), jnp.float32)
    _, prev = lax.scan(step, init, (chunk_states.transpose(1, 0, 2, 3, 4),
                                    chunk_decay.transpose(2, 0, 1)))
    prev = prev.transpose(1, 0, 2, 3, 4)
    y_off = jnp.einsum('bclhn,bchpn,bhcl->bclhp', cc, prev, jnp.exp(a_cs))
    y = (y_diag + y_off).reshape(bsz, t, SSD_HEADS, SSD_HEAD_DIM) + xs * d_skip.astype(jnp.float32)[:, None]
    g = y.reshape(bsz, t, SSD_DIM) * jax.nn.silu(z.astype(jnp.float32))
    g = g.reshape(bsz, t, SSD_GROUPS, SSD_DIM // SSD_GROUPS)
    g = g * lax.rsqrt(jnp.mean(g * g, axis=-1, keepdims=True) + EPS)
    return (g.reshape(bsz, t, SSD_DIM) * norm_w.astype(jnp.float32)).astype(z.dtype)

def gdn_mixer(qkv, z, b, a, conv_w, dt_bias, a_log, norm_w):
    bsz, t = qkv.shape[0], qkv.shape[1]
    nc = t // CHUNK
    qkv = jax.nn.silu(causal_dwconv(qkv, conv_w)).astype(jnp.float32)
    q, k, v = jnp.split(qkv, [GDN_KDIM, 2 * GDN_KDIM], axis=-1)
    q = l2norm(q.reshape(bsz, t, GDN_HEADS, GDN_HEAD_K)) * (GDN_HEAD_K ** -0.5)
    k = l2norm(k.reshape(bsz, t, GDN_HEADS, GDN_HEAD_K))
    v = v.reshape(bsz, t, GDN_HEADS, GDN_HEAD_V)
    beta = jax.nn.sigmoid(b.astype(jnp.float32))
    g = -jnp.exp(a_log.astype(jnp.float32)) * jax.nn.softplus(a.astype(jnp.float32) + dt_bias.astype(jnp.float32))

    def chunks(u):
        return u.reshape(bsz, nc, CHUNK, GDN_HEADS, u.shape[-1]).transpose(0, 3, 1, 2, 4)

    qc, kc, vc = chunks(q), chunks(k), chunks(v)
    betac = beta.reshape(bsz, nc, CHUNK, GDN_HEADS).transpose(0, 3, 1, 2)
    gc = jnp.cumsum(g.reshape(bsz, nc, CHUNK, GDN_HEADS).transpose(0, 3, 1, 2), axis=-1)
    decay = lower_exp_diff(gc)
    kbeta = kc * betac[..., None]
    strict = jnp.tril(jnp.einsum('bhcid,bhcjd->bhcij', kbeta, kc) * decay, -1)
    rhs = jnp.concatenate([vc * betac[..., None], kbeta * jnp.exp(gc)[..., None]], axis=-1)
    sol = lax.linalg.triangular_solve(strict, rhs, left_side=True, lower=True, unit_diagonal=True)
    u, w = jnp.split(sol, [GDN_HEAD_V], axis=-1)
    qk = jnp.einsum('bhcid,bhcjd->bhcij', qc, kc) * decay

    def step(state, inp):
        q_i, k_i, u_i, w_i, qk_i, g_i = inp
        v_new = u_i - jnp.einsum('bhld,bhde->bhle', w_i, state)
        o = (jnp.einsum('bhld,bhde->bhle', q_i * jnp.exp(g_i)[..., None], state)
             + jnp.einsum('bhls,bhse->bhle', qk_i, v_new))
        g_last = g_i[..., -1]
        state = (state * jnp.exp(g_last)[..., None, None]
                 + jnp.einsum('bhld,bhle->bhde', k_i * jnp.exp(g_last[..., None] - g_i)[..., None], v_new))
        return state, o

    xs = tuple(jnp.moveaxis(u_, 2, 0) for u_ in (qc, kc, u, w, qk, gc))
    init = jnp.zeros((bsz, GDN_HEADS, GDN_HEAD_K, GDN_HEAD_V), jnp.float32)
    _, o = lax.scan(step, init, xs)
    o = o.transpose(1, 0, 3, 2, 4).reshape(bsz, t, GDN_HEADS, GDN_HEAD_V)
    o = o * lax.rsqrt(jnp.mean(o * o, axis=-1, keepdims=True) + EPS) * norm_w.astype(jnp.float32)
    o = o * jax.nn.silu(z.astype(jnp.float32).reshape(bsz, t, GDN_HEADS, GDN_HEAD_V))
    return o.reshape(bsz, t, GDN_DIM).astype(z.dtype)

def second_inputs(seed: int = 0) -> dict:
    key = jax.random.key(seed)
    ks = jax.random.split(key, 24)
    L = DEPTH

    def nrm(k, shape, scale):
        return jax.random.normal(k, shape, jnp.float32) * scale

    def gain(k, shape):
        return 1.0 + 0.05 * jax.random.normal(k, shape, jnp.float32)

    def dt_bias_init(k, shape):
        u = jax.random.uniform(k, shape, jnp.float32, math.log(1e-3), math.log(1e-1))
        dtv = jnp.exp(u)
        return dtv + jnp.log(-jnp.expm1(-dtv))

    def a_log_init(k, shape):
        return jnp.log(jax.random.uniform(k, shape, jnp.float32, 1.0, 16.0))

    return {
        "x": nrm(ks[0], (BATCH, SEQ, D_MODEL), 1.0),
        "pre_mix_norm": gain(ks[1], (L, D_MODEL)),
        "post_mix_norm": gain(ks[2], (L, D_MODEL)),
        "pre_ffn_norm": gain(ks[3], (L, D_MODEL)),
        "post_ffn_norm": gain(ks[4], (L, D_MODEL)),
        "w_in": nrm(ks[5], (L, D_MODEL, IN_COLS), D_MODEL ** -0.5),
        "w_out": nrm(ks[6], (L, D_MIX, D_MODEL), D_MIX ** -0.5),
        "attn_sinks": nrm(ks[7], (L, ATT_HEADS), 0.5),
        "ssd_conv_w": nrm(ks[8], (L, CONV_K_2, SSD_CONV_DIM), CONV_K_2 ** -0.5),
        "ssd_conv_b": nrm(ks[9], (L, SSD_CONV_DIM), 0.01),
        "ssd_dt_bias": dt_bias_init(ks[10], (L, SSD_HEADS)),
        "ssd_A_log": a_log_init(ks[11], (L, SSD_HEADS)),
        "ssd_D": 1.0 + 0.1 * jax.random.normal(ks[12], (L, SSD_HEADS), jnp.float32),
        "ssd_norm_w": gain(ks[13], (L, SSD_DIM)),
        "gdn_conv_w": nrm(ks[14], (L, CONV_K_2, GDN_CONV_DIM), CONV_K_2 ** -0.5),
        "gdn_dt_bias": dt_bias_init(ks[15], (L, GDN_HEADS)),
        "gdn_A_log": a_log_init(ks[16], (L, GDN_HEADS)),
        "gdn_norm_w": gain(ks[17], (L, GDN_HEAD_V)),
        "ffn_w_gate": nrm(ks[18], (L, D_MODEL, FF), D_MODEL ** -0.5),
        "ffn_w_up": nrm(ks[19], (L, D_MODEL, FF), D_MODEL ** -0.5),
        "ffn_w_down": nrm(ks[20], (L, FF, D_MODEL), FF ** -0.5),
    }

def second_block(x, pre_mix_norm, post_mix_norm, pre_ffn_norm, post_ffn_norm, w_in, w_out,
              attn_sinks, ssd_conv_w, ssd_conv_b, ssd_dt_bias, ssd_A_log, ssd_D, ssd_norm_w,
              gdn_conv_w, gdn_dt_bias, gdn_A_log, gdn_norm_w, ffn_w_gate, ffn_w_up, ffn_w_down):
    offs = _offsets(IN_SIZES_2)
    for l in range(DEPTH):
        h = rmsnorm(x, pre_mix_norm[l])
        proj = h @ w_in[l]
        (a_q, a_k, a_v, s_z, s_xbc, s_dt, g_qkv, g_z, g_b, g_a) = jnp.split(proj, offs, axis=-1)
        att = swa_sink_alibi(a_q, a_k, a_v, attn_sinks[l])
        ssd = ssd_mixer(s_z, s_xbc, s_dt, ssd_conv_w[l], ssd_conv_b[l], ssd_dt_bias[l],
                        ssd_A_log[l], ssd_D[l], ssd_norm_w[l])
        gdn = gdn_mixer(g_qkv, g_z, g_b, g_a, gdn_conv_w[l], gdn_dt_bias[l], gdn_A_log[l], gdn_norm_w[l])
        mix = jnp.concatenate([att, ssd, gdn], axis=-1) @ w_out[l]
        x = x + rmsnorm(mix, post_mix_norm[l])
        h = rmsnorm(x, pre_ffn_norm[l])
        f = (jax.nn.silu(h @ ffn_w_gate[l]) * (h @ ffn_w_up[l])) @ ffn_w_down[l]
        x = x + rmsnorm(f, post_ffn_norm[l])
    return x


def setup_inputs(seed=0):
    out = dict(first_inputs(seed))
    for name, value in second_inputs(seed + 1).items():
        if name != "x":
            out[name + "_2"] = value
    return out


def reference(
    x, pre_norm_g, w_in, pool_w, pool_scale, conv_w, conv_b, w_branch, w_out, post_norm_g,
    pre_mix_norm_2, post_mix_norm_2, pre_ffn_norm_2, post_ffn_norm_2, w_in_2, w_out_2,
    attn_sinks_2, ssd_conv_w_2, ssd_conv_b_2, ssd_dt_bias_2, ssd_A_log_2, ssd_D_2, ssd_norm_w_2,
    gdn_conv_w_2, gdn_dt_bias_2, gdn_A_log_2, gdn_norm_w_2, ffn_w_gate_2, ffn_w_up_2,
    ffn_w_down_2,
):
    x = first_block(
        x, pre_norm_g, w_in, pool_w, pool_scale, conv_w, conv_b, w_branch, w_out, post_norm_g,
    )
    return second_block(
        x, pre_mix_norm_2, post_mix_norm_2, pre_ffn_norm_2, post_ffn_norm_2, w_in_2, w_out_2,
        attn_sinks_2, ssd_conv_w_2, ssd_conv_b_2, ssd_dt_bias_2, ssd_A_log_2, ssd_D_2,
        ssd_norm_w_2, gdn_conv_w_2, gdn_dt_bias_2, gdn_A_log_2, gdn_norm_w_2, ffn_w_gate_2,
        ffn_w_up_2, ffn_w_down_2,
    )


_drawn_inputs = setup_inputs


def setup_inputs(seed=0):
    import zlib

    import numpy as np

    out = dict(_drawn_inputs(seed))
    spreads = {}
    factors = {'conv_b': 8.0,
     'attn_sinks_2': 22.833,
     'ssd_conv_b_2': 6.991,
     'gdn_norm_w_2': 4.426,
     'ssd_D_2': 4.028,
     'ssd_norm_w_2': 3.464}
    for name, (base, spread) in spreads.items():
        noise = np.random.default_rng([zlib.crc32(name.encode()), seed]).standard_normal(out[name].shape)
        drawn = base * np.exp(spread * noise) if base else spread * noise
        out[name] = __import__('jax').numpy.asarray(drawn.astype(out[name].dtype))
    for name, factor in factors.items():
        out[name] = (out[name] * factor).astype(out[name].dtype)
    return out
```

```python
from contextlib import ExitStack

import concourse.bass as bass
from concourse import mybir

F32 = mybir.dt.float32
F32R = mybir.dt.float32r
ALU = mybir.AluOpType
ACT = mybir.ActivationFunctionType
AX = mybir.AxisListType.X

P = 128
T = 1024
D = 1024
NT = T // P
KC = D // P
HALF = 512
BW = D // 2
NC4 = BW // P
EPS = 1e-6
POOL_W = (2, 4, 8, 16)
TAPS = 3
SB_SCALE = 64 ** -0.5
EXP_LN_SET = 6

STEPS = [(qt, h, kb) for qt in range(2) for h in range(2) for kb in reversed(range(4 * (qt + 1)))]
NS = len(STEPS)
SECTIONS = 7
PAR = 5 + 5 + 16


def copy(pool, out, src, zero):
    shape = list(out.shape)
    none = zero[:] if len(shape) == 2 else zero[:].unsqueeze(1)
    return pool.tensor_tensor(out, src, none.to_broadcast(shape), ALU.subtract)


def weights_pass(pe, out, lhs, rhs, first, last):
    return pe.matmul(out, lhs, rhs, start=first, stop=last, skip_group_check=True)


class Stream:

    def __init__(self, nc, ctx, units):
        self.units = units
        self.raw = [ctx.enter_context(nc.sbuf_tensor(f"w_raw{s}", [P, 1024], F32)) for s in range(2)]
        self.hi = [ctx.enter_context(nc.sbuf_tensor(f"w_hi{s}", [P, 1024], F32R)) for s in range(2)]
        self.lo = [ctx.enter_context(nc.sbuf_tensor(f"w_lo{s}", [P, 1024], F32R)) for s in range(2)]
        self.loaded = [ctx.enter_context(nc.semaphore(f"w_loaded{s}")) for s in range(2)]
        self.hi_done = ctx.enter_context(nc.semaphore("w_hi_done"))
        self.lo_done = ctx.enter_context(nc.semaphore("w_lo_done"))

    def load(self, sp, c, k=0, i=0):
        if c >= 2:
            sp.wait_ge(self.lo_done, c - 1 + k * i)
        sp.dma_start(self.raw[c % 2][:], self.units[c + k * i]).then_inc(self.loaded[c % 2], 16)

    def split_hi(self, act, c, k=0, i=0, dest=None):
        act.wait_ge(self.loaded[c % 2], 16 * (c // 2 + 1) + 8 * k * i)
        act.copy(self.hi[c % 2][:] if dest is None else dest, self.raw[c % 2][:]).then_inc(self.hi_done, 1)

    def split_lo(self, dve, c, k=0, i=0, dest=None, hi=None):
        dve.wait_ge(self.hi_done, c + 1 + k * i)
        hi = self.hi[c % 2][:] if hi is None else hi
        dve.tensor_tensor(self.lo[c % 2][:] if dest is None else dest, self.raw[c % 2][:],
                          hi.bitcast(F32), ALU.subtract).then_inc(self.lo_done, 1)


def first_norm(nc, C, x_in, g, hT_hi, hT_lo):
    with ExitStack() as ctx:
        sb = lambda n, s, d=F32: ctx.enter_context(nc.sbuf_tensor(f"n0_{n}", s, d))
        sem = lambda n: ctx.enter_context(nc.semaphore(f"n0_{n}"))
        NX = 4
        x = [sb(f"x{s}", [P, D]) for s in range(NX)]
        junk, gain, st = sb("junk", [P, D]), sb("gain", [P, D]), sb("stat", [P, NT, 4])
        h = [sb(f"h{s}", [P, D]) for s in range(2)]
        pt = [ctx.enter_context(nc.psum_tensor(f"n0_pt{s}", [P, D], F32)) for s in range(2)]
        x_here = [sem(f"x_here{s}") for s in range(NX)]
        g_here, sq, ms, rt, rc = sem("g_here"), sem("sq"), sem("ms"), sem("rt"), sem("rc")
        h_ready, t_done, hi_done, lo_done = sem("h_ready"), sem("t_done"), sem("hi_done"), sem("lo_done")
        x_t = x_in.rearrange("(t p) d -> t p d", p=P)
        tok = lambda t: slice(t * P, (t + 1) * P)

        with nc.Block() as block:
            @block.sync
            def _(sp):
                for t in range(NT):
                    if t >= NX:
                        sp.wait_ge(h_ready, t - NX + 1)
                    sp.dma_start(x[t % NX][:], x_t[t]).then_inc(x_here[t % NX], 16)
                    if t == 0:
                        sp.dma_start(gain[:], g.to_broadcast([P, D])).then_inc(g_here, 16)

            @block.scalar
            def _(act):
                def high(t):
                    act.wait_ge(t_done, t + 1)
                    act.copy(hT_hi[:, :, tok(t)], pt[t % 2][:].rearrange("p (k t) -> p k t", k=KC)).then_inc(hi_done, 1)

                for t in range(NT):
                    act.wait_ge(x_here[t % NX], 16 * (t // NX + 1))
                    act.activation(junk[:], x[t % NX][:], ACT.Square, accum_out=st[:, t, 0:1]).then_inc(sq, 1)
                    act.wait_ge(ms, t + 1)
                    act.activation(st[:, t, 2:3], st[:, t, 1:2], ACT.Sqrt).then_inc(rt, 1)
                    if t >= 2:
                        high(t - 2)
                high(NT - 2)
                high(NT - 1)

            @block.vector
            def _(dve):
                def low(t):
                    dve.wait_ge(hi_done, t + 1)
                    dve.tensor_tensor(hT_lo[:, :, tok(t)], pt[t % 2][:].rearrange("p (k t) -> p k t", k=KC),
                                      hT_hi[:, :, tok(t)].bitcast(F32), ALU.subtract).then_inc(lo_done, 1)

                dve.wait_ge(g_here, 16)
                for t in range(NT):
                    dve.wait_ge(sq, t + 1)
                    dve.tensor_scalar(st[:, t, 1:2], st[:, t, 0:1], 1.0 / D, EPS, ALU.mult, ALU.add).then_inc(ms, 1)
                    if t >= 3:
                        low(t - 3)
                    dve.wait_ge(rt, t + 1)
                    dve.reciprocal(st[:, t, 3:4], st[:, t, 2:3]).then_inc(rc, 1)
                    dve.wait_ge(rc, t + 1)
                    if t >= 2:
                        dve.wait_ge(t_done, t - 1)
                    dve.scalar_tensor_tensor(h[t % 2][:], x[t % NX][:], st[:, t, 3:4], gain[:], ALU.mult, ALU.mult).then_inc(h_ready, 1)
                for t in range(NT - 3, NT):
                    low(t)

            @block.tensor
            def _(pe):
                for t in range(NT):
                    pe.wait_ge(h_ready, t + 1)
                    if t >= 2:
                        pe.wait_ge(lo_done, t - 1)
                    for k in range(KC):
                        mm = pe.transpose(pt[t % 2][:, k * P:(k + 1) * P], h[t % 2][:, k * P:(k + 1) * P], C["ident"][:])
                    mm.then_inc(t_done, 1)


def layer1_mixers(nc, C, W, hT_hi, hT_lo, chan, pool_w, y_out):
    with ExitStack() as ctx:
        sb = lambda n, s, d=F32: ctx.enter_context(nc.sbuf_tensor(n, s, d))
        sem = lambda n: ctx.enter_context(nc.semaphore(n))
        q_next, k_next, v_next = sb("q_next", [P, T]), sb("k_next", [P, T]), sb("v_next", [P, T])
        q_cur, k_cur = sb("q_cur", [P, T]), sb("k_cur", [P, T])
        v_tok = sb("v_tok", [P, NT * P])
        tmp = [sb(f"sb_tmp{s}", [P, HALF]) for s in range(2)]
        sp_t = [sb(f"sb_sp{s}", [P, HALF]) for s in range(2)]
        w_t = [sb(f"sb_w{s}", [P, HALF]) for s in range(2)]
        later = [sb(f"sb_later{s}", [P, HALF]) for s in range(2)]
        PAD = 16
        pv = [sb(f"pool_v{s}", [P, PAD + T]) for s in range(3)]
        cz = sb("conv_z", [P, 2 + T])
        cx, cgb = sb("conv_x", [P, T]), sb("conv_gb", [P, T])
        y = [sb(f"y{b}", [P, T]) for b in range(3)]
        par, pw = sb("chan_par", [P, PAR]), sb("pool_w_c", [P, P])
        zero = sb("sb_zero", [P, 1])
        A = [ctx.enter_context(nc.psum_tensor(f"psA{s}", [P, HALF], F32)) for s in range(3)]
        O = ctx.enter_context(nc.psum_tensor("psO", [P, HALF], F32))
        G = [ctx.enter_context(nc.psum_tensor(f"psG{s}", [P, T], F32)) for s in range(2)]

        qk_done, sp_ready, tri_done, w_masked, pv_done = (sem(n) for n in ("qk_done", "sp_ready", "tri_done", "w_masked", "pv_done"))
        abs_done, exp_done, ln_done, sp_raw, exp2_done, later_ready = (
            sem(n) for n in ("abs_done", "exp_done", "ln_done", "sp_raw", "exp2_done", "later_ready"))
        o_read, g_full = sem("o_read"), sem("g_full")
        g_evac = [sem(f"g_evac{s}") for s in range(2)]
        q_copied, k_copied = sem("q_copied"), sem("k_copied")
        par_here = sem("par_here")
        pool_step, pooled, conv_step, conv_done = sem("pool_step"), sem("pooled"), sem("conv_step"), sem("conv_done")
        y_stored = [sem(f"y{b}_stored") for b in range(3)]
        pads = sem("pads")

        SBG, POOLV, POOLG, CX, CGC, CGB, CG, QN, KN, VN = range(10)
        U0, UI, GI = 3, 10, 12
        PM = 1 + CG
        entry_of = lambda j: 1 + j + (j >= CG)
        BUF = [0, 1, 0] + [0, 1, 0, 1, 0, 1, 0, 0, 1, 0, 1, 0]
        BEFORE = [BUF[:c].count(b) for c, b in enumerate(BUF)]
        PER = [BUF[U0:].count(b) for b in range(2)]
        ND = [sum(P * kb >= HALF * qt for qt, _, kb in STEPS[:s]) for s in range(NS + 1)]
        NL = [sum(kb > 0 for _, _, kb in STEPS[:s]) for s in range(NS + 1)]

        def first_query(s):
            qt, h, kb = STEPS[s]
            return max(0, P * kb - HALF * qt)

        def diagonal(s):
            qt, h, kb = STEPS[s]
            return P * kb >= HALF * qt

        def groups(nu):
            per = nu * 24 // NS
            return [(s * per, (s + 1) * per) for s in range(NS)]

        def finished(nu, s):
            first, last = groups(nu)[s]
            return [g // 24 for g in range(first, last) if g % 24 == 23]

        def entry_free(eng, c, i=0):
            if BEFORE[c]:
                eng.wait_ge(g_evac[BUF[c]], BEFORE[c] + PER[BUF[c]] * i)

        def entry_full(eng, c, i=0):
            eng.wait_ge(g_full, c + 1 + GI * i)

        def entry_out(eng, c, i=0):
            eng.wait_ge(g_evac[BUF[c]], BEFORE[c] + 1 + PER[BUF[c]] * i)

        def unit_products(pe, c, g, first, last):
            for n in range(first, last):
                kc, p = divmod(n, 3)
                lhs = (W.lo if p == 0 else W.hi)[c % 2][:, kc * P:(kc + 1) * P]
                rhs = hT_lo if p == 1 else hT_hi
                for hf in range(2):
                    mm = weights_pass(pe, g[:, hf * HALF:(hf + 1) * HALF], lhs, rhs[:, kc, hf * HALF:(hf + 1) * HALF],
                                      n == 0, n == 23)
            return mm

        with nc.Block() as block:
            @block.sync
            def _(sp):
                def start(i):
                    sp.dma_start(par[:], chan[i]).then_inc(par_here, 16)
                    sp.dma_start(pw[:], pool_w[i]).then_inc(par_here, 16)

                def store(i):
                    entry_out(sp, U0 + PM, i)
                    sp.dma_start(y_out[i], y[0][:]).then_inc(y_stored[0], 16)
                    sp.wait_ge(conv_done, i + 1)
                    sp.dma_start(y_out[NC4 + i], y[1][:]).then_inc(y_stored[1], 16)
                    sp.wait_ge(o_read, 2 * i + 2)
                    sp.dma_start(y_out[2 * NC4 + i], y[2][:]).then_inc(y_stored[2], 16)

                for c in range(2, 5):
                    W.load(sp, c)
                with sp.Fori(0, NC4 - 1) as i:
                    start(i)
                    for j in range(UI):
                        W.load(sp, U0 + 2 + j, UI, i)
                    store(i)
                start(NC4 - 1)
                for j in range(SECTIONS):
                    W.load(sp, U0 + 2 + UI * (NC4 - 1) + j)
                store(NC4 - 1)
                for b in range(3):
                    sp.wait_ge(y_stored[b], 16 * NC4)

            @block.gpsimd
            def _(pool):
                pool.wait_ge(pads, 5)
                with pool.Fori(0, NC4) as i:
                    pool.wait_ge(qk_done, NS * i)
                    entry_out(pool, 0, i)
                    copy(pool, q_cur[:], q_next[:], zero).then_inc(q_copied, 1)
                    entry_out(pool, 1, i)
                    copy(pool, k_cur[:], k_next[:], zero).then_inc(k_copied, 1)
                    for s, (qt, h, kb) in enumerate(STEPS):
                        if kb == 0:
                            continue
                        q0 = first_query(s)
                        src, dst, sp_s = later[s % 2], later[(s + 1) % 2], sp_t[s % 2]
                        pool.wait_ge(sp_ready, NS * i + s + 1)
                        pool.wait_ge(tri_done, NS * i + s)
                        if kb == 4 * qt + 3:
                            copy(pool, dst[:, q0:], sp_s[:, q0:], zero).then_inc(later_ready, 1)
                            continue
                        pool.wait_ge(later_ready, NL[NS] * i + NL[s])
                        if diagonal(s):
                            copy(pool, dst[:, q0:q0 + P], sp_s[:, q0:q0 + P], zero)
                            q0 += P
                        pool.tensor_tensor(dst[:, q0:], src[:, q0:], sp_s[:, q0:], ALU.add).then_inc(later_ready, 1)

            @block.scalar
            def _(act):
                def exp_ln_tables():
                    act.add_instruction(mybir.InstLoadActFuncSet(name=nc.get_next_instruction_name(),
                                                                 act_func_set_id=EXP_LN_SET))

                def softplus_parts(i, s):
                    a, t = A[s % 3][:, first_query(s):], tmp[s % 2][:, first_query(s):]
                    act.wait_ge(qk_done, NS * i + s + 1)
                    act.wait_ge(sp_ready, NS * i + max(s - 1, 0))
                    act.activation(t, a, ACT.Abs).then_inc(abs_done, 1)
                    act.wait_ge(abs_done, NS * i + s + 1)
                    act.activation(t, t, ACT.Exp, scale=-1.0).then_inc(exp_done, 1)
                    act.wait_ge(exp_done, NS * i + s + 1)
                    act.activation(t, t, ACT.Ln, bias=1.0).then_inc(ln_done, 1)

                def weights(i, s):
                    act.wait_ge(tri_done, NS * i + s + 1)
                    act.wait_ge(pv_done, NS * i + max(s - 1, 0))
                    act.activation(w_t[s % 2][:, first_query(s):], A[s % 3][:, first_query(s):], ACT.Exp).then_inc(exp2_done, 1)

                def stage(c, i=0):
                    if c == 0:
                        act.wait_ge(q_copied, i)
                        act.mul(q_next[:], G[0][:], SB_SCALE).then_inc(g_evac[0], 1)
                    elif c == 1:
                        act.wait_ge(k_copied, i)
                        act.copy(k_next[:], G[1][:]).then_inc(g_evac[1], 1)
                    else:
                        act.copy(v_next[:], G[0][:]).then_inc(g_evac[0], 1)

                def evacuate(i, j):
                    c = U0 + entry_of(j)
                    g, out = G[BUF[c]], g_evac[BUF[c]]
                    if j == CGC:
                        return
                    entry_full(act, c, i)
                    if j in (SBG, POOLG, CG):
                        b = {POOLG: 0, CG: 1, SBG: 2}[j]
                        act.wait_ge(y_stored[b], 16 * i)
                        act.activation(y[b][:], g[:], ACT.Silu).then_inc(out, 1)
                        exp_ln_tables()
                    elif j == POOLV:
                        act.wait_ge(pooled, 2 * i)
                        act.copy(pv[0][:, PAD:], g[:]).then_inc(out, 1)
                    elif j == CX:
                        act.wait_ge(conv_done, i)
                        act.copy(cx[:], g[:]).then_inc(out, 1)
                    elif j == CGB:
                        act.wait_ge(conv_done, i)
                        act.copy(cgb[:], g[:]).then_inc(out, 1)
                    else:
                        stage(j - QN, i + 1)

                def iteration(i, nu):
                    for s in range(NS):
                        softplus_parts(i, s)
                        if s >= 1:
                            weights(i, s - 1)
                        for j in finished(nu, s):
                            evacuate(i, j)
                            if j + 2 < nu or nu == UI:
                                entry_full(act, U0 + entry_of(j), i)
                                W.split_hi(act, U0 + 2 + j, UI, i)
                    weights(i, NS - 1)

                W.split_hi(act, 0)
                W.split_hi(act, 1)
                for c in range(3):
                    entry_full(act, c)
                    W.split_hi(act, c + 2)
                    stage(c)
                exp_ln_tables()
                with act.Fori(0, NC4 - 1) as i:
                    iteration(i, UI)
                iteration(NC4 - 1, SECTIONS)

            @block.vector
            def _(dve):
                def softplus(i, s):
                    q0 = first_query(s)
                    out = sp_t[s % 2]
                    dve.wait_ge(ln_done, NS * i + s + 1)
                    dve.wait_ge(tri_done, NS * i + max(s - 1, 0))
                    dve.wait_ge(later_ready, NL[NS] * i + (NL[s - 1] if s >= 1 else 0))
                    ins = dve.scalar_tensor_tensor(out[:, q0:], A[s % 3][:, q0:], 0.0, tmp[s % 2][:, q0:], ALU.max, ALU.add)
                    if diagonal(s):
                        ins.then_inc(sp_raw, 1)
                        dve.wait_ge(sp_raw, ND[NS] * i + ND[s] + 1)
                        ins = dve.tensor_tensor(out[:, q0:q0 + P], out[:, q0:q0 + P], C["before"][:], ALU.mult)
                    ins.then_inc(sp_ready, 1)

                def mask_weights(i, s):
                    if diagonal(s):
                        w = w_t[s % 2][:, first_query(s):first_query(s) + P]
                        dve.wait_ge(exp2_done, NS * i + s + 1)
                        dve.tensor_tensor(w, w, C["before"][:], ALU.mult).then_inc(w_masked, 1)

                def attention_out(i, qt):
                    entry_out(dve, U0 + entry_of(SBG), i)
                    dve.wait_ge(pv_done, NS * i + (8 if qt == 0 else NS))
                    v = y[2][:, qt * HALF:(qt + 1) * HALF]
                    dve.tensor_tensor(v, O[:], v, ALU.mult).then_inc(o_read, 1)

                def turn_v(i):
                    entry_full(dve, U0, i)
                    dve.wait_ge(pv_done, NS * i)
                    dve.tensor_copy(v_tok[:], G[BUF[U0]][:]).then_inc(g_evac[BUF[U0]], 1)

                def pool_windows(i):
                    entry_out(dve, U0 + entry_of(POOLV), i)
                    dve.wait_ge(par_here, 32 * i + 32)
                    src = pv[0]
                    for n in range(4):
                        dst = pv[1 + n % 2]
                        dve.scalar_tensor_tensor(dst[:, PAD:], src[:, PAD - 2 ** n:PAD - 2 ** n + T], par[:, 5 + n:6 + n],
                                                 src[:, PAD:], ALU.mult, ALU.add).then_inc(pool_step, 1)
                        dve.wait_ge(pool_step, 4 * i + n + 1)
                        src = dst
                    dve.tensor_tensor(pv[1][:, PAD:PAD + 16], src[:, PAD:PAD + 16], par[:, 10:26], ALU.mult)
                    dve.tensor_scalar(pv[1][:, PAD + 16:], src[:, PAD + 16:], par[:, 9:10], None, ALU.mult).then_inc(pooled, 1)
                    dve.wait_ge(pooled, 2 * i + 1)
                    dve.tensor_tensor(pv[1][:, PAD:], pv[1][:, PAD:], pv[0][:, PAD:], ALU.subtract).then_inc(pooled, 1)

                def gate_pool(i):
                    c = U0 + PM
                    entry_full(dve, c, i)
                    entry_out(dve, U0 + entry_of(POOLG), i)
                    dve.scalar_tensor_tensor(y[0][:], G[BUF[c]][:], par[:, 4:5], y[0][:], ALU.mult, ALU.mult).then_inc(g_evac[BUF[c]], 1)

                def conv_taps(i):
                    c = U0 + entry_of(CGC)
                    entry_full(dve, c, i)
                    entry_out(dve, U0 + entry_of(CX), i)
                    dve.wait_ge(par_here, 32 * i + 32)
                    dve.tensor_tensor(cz[:, 2:], G[BUF[c]][:], cx[:], ALU.mult).then_inc(g_evac[BUF[c]], 1)
                    entry_out(dve, c, i)
                    dve.tensor_scalar(cx[:], cz[:, 2:], par[:, 2:3], par[:, 3:4], ALU.mult, ALU.add).then_inc(conv_step, 1)
                    for n in range(2):
                        dve.wait_ge(conv_step, 4 * i + 1 + n)
                        dve.scalar_tensor_tensor(cx[:], cz[:, 1 - n:1 - n + T], par[:, 1 - n:2 - n], cx[:],
                                                 ALU.mult, ALU.add).then_inc(conv_step, 1)

                def gate_conv(i):
                    entry_out(dve, U0 + entry_of(CGB), i)
                    entry_out(dve, U0 + entry_of(CG), i)
                    dve.wait_ge(conv_step, 4 * i + 3)
                    dve.tensor_tensor(cx[:], cx[:], cgb[:], ALU.mult).then_inc(conv_step, 1)
                    dve.wait_ge(conv_step, 4 * i + 4)
                    dve.tensor_tensor(y[1][:], cx[:], y[1][:], ALU.mult).then_inc(conv_done, 1)

                def iteration(i, nu):
                    turn_v(i)
                    for s in range(NS):
                        softplus(i, s)
                        if s >= 1:
                            mask_weights(i, s - 1)
                        if s == 10:
                            attention_out(i, 0)
                        for j in finished(nu, s):
                            if j + 2 < nu or nu == UI:
                                W.split_lo(dve, U0 + 2 + j, UI, i)
                            if j == POOLV:
                                pool_windows(i)
                            if j == CGC:
                                conv_taps(i)
                            if j == CGB:
                                gate_pool(i)
                            if j == CG:
                                gate_conv(i)
                    mask_weights(i, NS - 1)
                    attention_out(i, 1)

                for s in range(3):
                    dve.memset(pv[s][:, 0:PAD], 0.0).then_inc(pads, 1)
                dve.memset(cz[:, 0:2], 0.0).then_inc(pads, 1)
                dve.memset(zero[:], 0.0).then_inc(pads, 1)
                for c in range(U0 + 2):
                    W.split_lo(dve, c)
                dve.wait_ge(pads, 5)
                with dve.Fori(0, NC4 - 1) as i:
                    iteration(i, UI)
                iteration(NC4 - 1, SECTIONS)

            @block.tensor
            def _(pe):
                def logits(i, s):
                    qt, h, kb = STEPS[s]
                    pe.wait_ge(exp2_done, NS * i + max(s - 2, 0))
                    pe.matmul(A[s % 3][:, first_query(s):], k_cur[64 * h:64 * h + 64, kb * P:(kb + 1) * P],
                              q_cur[64 * h:64 * h + 64, HALF * qt + first_query(s):HALF * (qt + 1)],
                              start=True, stop=True, skip_group_check=True).then_inc(qk_done, 1)

                def sums(i, s):
                    qt, h, kb = STEPS[s]
                    pe.wait_ge(sp_ready, NS * i + s + 1)
                    mm = pe.matmul(A[s % 3][:, first_query(s):], C["minus_from"][:], sp_t[s % 2][:, first_query(s):],
                                   start=False, stop=True, skip_group_check=True)
                    if kb < 4 * qt + 3:
                        q0 = max(0, P * (kb + 1) - HALF * qt)
                        pe.wait_ge(later_ready, NL[NS] * i + NL[s])
                        mm = pe.matmul(A[s % 3][:, q0:], C["minus_one"][:], later[s % 2][:, q0:],
                                       start=False, stop=True, skip_group_check=True)
                    mm.then_inc(tri_done, 1)

                def values(i, s):
                    qt, h, kb = STEPS[s]
                    if s == 0:
                        entry_out(pe, U0, i)
                    if s in (0, 8):
                        pe.wait_ge(o_read, 2 * i + (s == 8))
                    if diagonal(s):
                        pe.wait_ge(w_masked, ND[NS] * i + ND[s] + 1)
                    pe.wait_ge(exp2_done, NS * i + s + 1)
                    pe.matmul(O[64 * h:64 * h + 64, first_query(s):], v_tok[:, kb * P + 64 * h:kb * P + 64 * h + 64],
                              w_t[s % 2][:, first_query(s):], start=(kb == 4 * qt + 3), stop=(kb == 0),
                              skip_group_check=True).then_inc(pv_done, 1)

                def mix(i):
                    c = U0 + PM
                    entry_free(pe, c, i)
                    pe.wait_ge(pooled, 2 * i + 2)
                    for hf in range(2):
                        mm = pe.matmul(G[BUF[c]][:, hf * HALF:(hf + 1) * HALF], pw[:],
                                       pv[1][:, PAD + hf * HALF:PAD + (hf + 1) * HALF], start=True, stop=True)
                    mm.then_inc(g_full, 1)

                def projections(i, first, last):
                    for n in range(first, last):
                        j, g = divmod(n, 24)
                        c = U0 + entry_of(j)
                        if g == 0:
                            entry_free(pe, c, i)
                            pe.wait_ge(W.lo_done, U0 + j + 1 + UI * i)
                        mm = unit_products(pe, U0 + j, G[BUF[c]], g, g + 1)
                        if g == 23:
                            mm.then_inc(g_full, 1)

                def iteration(i, nu):
                    entry_free(pe, U0, i)
                    entry_out(pe, 2, i)
                    for kb in range(NT):
                        mm = pe.transpose(G[BUF[U0]][:, kb * P:(kb + 1) * P], v_next[:, kb * P:(kb + 1) * P], C["ident"][:])
                    mm.then_inc(g_full, 1)
                    pe.wait_ge(q_copied, i + 1)
                    pe.wait_ge(k_copied, i + 1)
                    for s in range(NS):
                        logits(i, s)
                        projections(i, *groups(nu)[s])
                        if s >= 1:
                            sums(i, s - 1)
                        if s >= 2:
                            values(i, s - 2)
                        if CGB in finished(nu, s):
                            mix(i)
                    sums(i, NS - 1)
                    values(i, NS - 2)
                    values(i, NS - 1)

                for c in range(U0):
                    entry_free(pe, c)
                    pe.wait_ge(W.lo_done, c + 1)
                    unit_products(pe, c, G[BUF[c]], 0, 24).then_inc(g_full, 1)
                with pe.Fori(0, NC4 - 1) as i:
                    iteration(i, UI)
                iteration(NC4 - 1, SECTIONS)


def layer1_merge(nc, W, U0, hT_hi, hT_lo, y_dram, merged):
    with ExitStack() as ctx:
        sb = lambda n, s, d=F32: ctx.enter_context(nc.sbuf_tensor(n, s, d))
        sem = lambda n: ctx.enter_context(nc.semaphore(n))
        y_raw = sb("mg_y", [P, NC4, T])
        y_hi, y_lo = sb("mg_y_hi", [P, NC4, T], F32R), sb("mg_y_lo", [P, NC4, T], F32R)
        gate = [sb(f"mg_gate{s}", [P, T]) for s in range(2)]
        prod = sb("mg_prod", [P, T])
        G = [ctx.enter_context(nc.psum_tensor(f"mg_ps{s}", [P, T], F32)) for s in range(2)]
        y_here, y_hi_done, y_lo_done = sem("mg_y_here"), sem("mg_y_hi_done"), sem("mg_y_lo_done")
        full, added, zeroed, prod_done = sem("mg_full"), sem("mg_added"), sem("mg_zeroed"), sem("mg_prod_done")
        evac = [sem(f"mg_evac{s}") for s in range(2)]
        UB, EB = 12, 16
        last_entry = lambda u: 4 * (u // 3) + (0, 1, 3)[u % 3]

        with nc.Block() as block:
            @block.sync
            def _(sp):
                with sp.Fori(0, 3) as n:
                    sp.wait_ge(y_lo_done, NC4 * n)
                    sp.dma_start(y_raw[:], y_dram[bass.ds(NC4 * n, NC4)].rearrange("c p t -> p c t")).then_inc(y_here, 16)
                    for u in range(UB):
                        W.load(sp, U0 + 2 + u, UB, n)

            @block.scalar
            def _(act):
                W.split_hi(act, U0)
                W.split_hi(act, U0 + 1)

                def branch(n, last):
                    act.wait_ge(y_here, 16 * n + 16)
                    act.wait_ge(full, EB * n)
                    for c in range(NC4):
                        act.copy(y_hi[:, c, :], y_raw[:, c, :]).then_inc(y_hi_done, 1)
                    for u in range(UB):
                        e = last_entry(u)
                        act.wait_ge(full, EB * n + e + 1)
                        if u + 2 < UB or not last:
                            W.split_hi(act, U0 + 2 + u, UB, n)
                        if u % 3 < 2:
                            m = 2 * (u // 3) + u % 3
                            act.wait_ge(added, KC * n + max(m - 1, 0))
                            act.activation(gate[m % 2][:], G[e % 2][:], ACT.Sigmoid).then_inc(evac[e % 2], 1)

                with act.Fori(0, 2) as n:
                    branch(n, False)
                branch(2, True)

            @block.vector
            def _(dve):
                dve.memset(merged[:], 0.0).then_inc(zeroed, 1)
                W.split_lo(dve, U0)
                W.split_lo(dve, U0 + 1)
                dve.wait_ge(zeroed, 1)

                def branch(n, last):
                    for c in range(NC4):
                        dve.wait_ge(y_hi_done, NC4 * n + c + 1)
                        dve.tensor_tensor(y_lo[:, c, :], y_raw[:, c, :], y_hi[:, c, :].bitcast(F32), ALU.subtract).then_inc(y_lo_done, 1)
                    for u in range(UB):
                        if u % 3 == 2:
                            for r in range(2):
                                e, m = 4 * (u // 3) + 2 + r, 2 * (u // 3) + r
                                dve.wait_ge(full, EB * n + e + 1)
                                dve.wait_ge(evac[m % 2], EB // 2 * n + (e - 2) // 2 + 1)
                                dve.wait_ge(added, KC * n + m)
                                dve.tensor_tensor(prod[:], G[e % 2][:], gate[m % 2][:], ALU.mult).then_inc(evac[e % 2], 1)
                                dve.wait_ge(evac[e % 2], EB // 2 * n + e // 2 + 1)
                                dve.tensor_tensor(merged[:, m, :], merged[:, m, :], prod[:], ALU.add).then_inc(added, 1)
                        if u + 2 < UB or not last:
                            W.split_lo(dve, U0 + 2 + u, UB, n)

                with dve.Fori(0, 2) as n:
                    branch(n, False)
                branch(2, True)

            @block.tensor
            def _(pe):
                with pe.Fori(0, 3) as n:
                    for u in range(UB):
                        s = (U0 + u) % 2
                        pe.wait_ge(W.lo_done, U0 + u + 1 + UB * n)
                        if u == 2:
                            pe.wait_ge(y_lo_done, NC4 * n + NC4)
                        for r in range(1 if u % 3 < 2 else 2):
                            e = last_entry(u) if u % 3 < 2 else 4 * (u // 3) + 2 + r
                            pe.wait_ge(evac[e % 2], EB // 2 * n + e // 2)
                            hi, lo, nk = (hT_hi, hT_lo, KC) if u % 3 < 2 else (y_hi, y_lo, NC4)
                            for k in range(nk):
                                cols = slice(k * P, (k + 1) * P) if u % 3 < 2 else slice(k * 2 * P + r * P, k * 2 * P + (r + 1) * P)
                                for p, (a, b) in enumerate(((W.lo, hi), (W.hi, lo), (W.hi, hi))):
                                    for hf in range(2):
                                        mm = weights_pass(pe, G[e % 2][:, hf * HALF:(hf + 1) * HALF], a[s][:, cols],
                                                          b[:, k, hf * HALF:(hf + 1) * HALF], k == 0 and p == 0, k == nk - 1 and p == 2)
                            mm.then_inc(full, 1)


def product_and_norms(nc, name, C, W, U0, xT, x_in, g_post, g_pre, x_out, hT_hi, hT_lo):
    with ExitStack() as ctx:
        sb = lambda n, s, d=F32: ctx.enter_context(nc.sbuf_tensor(f"{name}_{n}", s, d))
        sem = lambda n: ctx.enter_context(nc.semaphore(f"{name}_{n}"))
        NP = 3
        w_hi, w_lo = sb("w_hi", [P, KC, D], F32R), sb("w_lo", [P, KC, D], F32R)
        x = [sb(f"x{s}", [P, D]) for s in range(2)]
        gp, gn, st = sb("gpost", [P, D]), sb("gpre", [P, D]), sb("stat", [P, NT, 8])
        h, junk, add = [xT[:, s, :] for s in range(2)], xT[:, 2, :], [xT[:, 3 + s, :] for s in range(2)]
        ps = [ctx.enter_context(nc.psum_tensor(f"{name}_ps{t}", [P, D], F32)) for t in range(NP)]
        pt = ctx.enter_context(nc.psum_tensor(f"{name}_pt", [P, D], F32))
        x_hi_done, x_lo_done, full = sem("x_hi_done"), sem("x_lo_done"), sem("full")
        x_here = [sem(f"x_here{s}") for s in range(2)]
        x_kept = [sem(f"x_kept{s}") for s in range(2)]
        g_here, sq_o, sq_x, rt, rc, ms = (sem(n) for n in ("g_here", "sq_o", "sq_x", "rt", "rc", "ms"))
        scaled, x_new, h_ready, t_done, hi_done, lo_done = (sem(n) for n in ("scaled", "x_new", "h_ready", "t_done", "hi_done", "lo_done"))
        x_t = x_in.rearrange("(t p) d -> t p d", p=P)
        o_t = x_out.rearrange("(t p) d -> t p d", p=P)
        tok = lambda t: slice(t * P, (t + 1) * P)
        turned = pt[:].rearrange("p (k t) -> p k t", k=KC)

        ORDER = [(k, t - k) for t in range(NT + 2) for k in (2, 1, 0) if 0 <= t - k < NT]
        ROOT = {kt: n + 1 for n, kt in enumerate(kt for kt in ORDER if kt[0] < 2)}

        TURNS = {t: [t - NP] for t in range(NP, NP + 2)} | {t: [t - 3] for t in range(NP + 2, NT)}
        TURNS[NT - 1] = list(range(NT - 1 - 3, NT))

        with nc.Block() as block:
            @block.sync
            def _(sp):
                for k in range(KC):
                    W.load(sp, U0 + 2 + k)
                    if k == 2:
                        sp.dma_start(gp[:], g_post.to_broadcast([P, D])).then_inc(g_here, 16)
                        sp.dma_start(gn[:], g_pre.to_broadcast([P, D])).then_inc(g_here, 16)
                    if k in (3, 4):
                        sp.dma_start(x[k - 3][:], x_t[k - 3]).then_inc(x_here[k - 3], 16)
                for t in range(NT):
                    sp.wait_ge(x_new, t + 1)
                    sp.dma_start(o_t[t], x[t % 2][:]).then_inc(x_kept[t % 2], 16)
                    if t + 2 < NT:
                        sp.wait_ge(x_kept[t % 2], 16 * (t // 2 + 1))
                        sp.wait_ge(h_ready, t + 1)
                        sp.dma_start(x[t % 2][:], x_t[t + 2]).then_inc(x_here[t % 2], 16)
                for b in range(2):
                    sp.wait_ge(x_kept[b], 16 * (NT // 2))

            @block.scalar
            def _(act):
                def root(k, t):
                    act.wait_ge(ms, ROOT[k, t])
                    act.activation(st[:, t, 4 * k + 2:4 * k + 3], st[:, t, 4 * k + 1:4 * k + 2], ACT.Sqrt).then_inc(rt, 1)

                for k in range(KC):
                    act.copy(hT_hi[:, k, :], xT[:, k, :]).then_inc(x_hi_done, 1)
                    W.split_hi(act, U0 + k, dest=w_hi[:, k, :])
                act.wait_ge(x_lo_done, KC)
                for k, t in ORDER:
                    if k == 0:
                        act.wait_ge(full, t + 1)
                        act.activation(junk, ps[t % NP][:], ACT.Square, accum_out=st[:, t, 0:1]).then_inc(sq_o, 1)
                        root(0, t)
                    elif k == 1:
                        act.wait_ge(x_new, t + 1)
                        act.activation(junk, x[t % 2][:], ACT.Square, accum_out=st[:, t, 4:5]).then_inc(sq_x, 1)
                        root(1, t)
                    else:
                        act.wait_ge(t_done, t + 1)
                        act.copy(hT_hi[:, :, tok(t)], turned).then_inc(hi_done, 1)

            @block.vector
            def _(dve):
                def inverse_root(k, t, sq):
                    s = lambda n: st[:, t, 4 * k + n:4 * k + n + 1]
                    dve.wait_ge(sq, t + 1)
                    dve.tensor_scalar(s(1), s(0), 1.0 / D, EPS, ALU.mult, ALU.add).then_inc(ms, 1)
                    dve.wait_ge(rt, ROOT[k, t])
                    dve.reciprocal(s(3), s(2)).then_inc(rc, 1)
                    dve.wait_ge(rc, ROOT[k, t])
                    return s(3)

                for k in range(KC):
                    dve.wait_ge(x_hi_done, k + 1)
                    dve.tensor_tensor(hT_lo[:, k, :], xT[:, k, :], hT_hi[:, k, :].bitcast(F32), ALU.subtract).then_inc(x_lo_done, 1)
                    W.split_lo(dve, U0 + k, dest=w_lo[:, k, :], hi=w_hi[:, k, :])
                dve.wait_ge(x_lo_done, KC)
                dve.wait_ge(g_here, 32)
                for k, t in ORDER:
                    b = t % 2
                    if k == 0:
                        r = inverse_root(0, t, sq_o)
                        if t >= 2:
                            dve.wait_ge(x_new, t - 1)
                        dve.scalar_tensor_tensor(add[b], ps[t % NP][:], r, gp[:], ALU.mult, ALU.mult).then_inc(scaled, 1)
                        dve.wait_ge(scaled, t + 1)
                        dve.wait_ge(x_here[b], 16 * (t // 2 + 1))
                        dve.tensor_tensor(x[b][:], x[b][:], add[b], ALU.add).then_inc(x_new, 1)
                    elif k == 1:
                        r = inverse_root(1, t, sq_x)
                        if t >= 2:
                            dve.wait_ge(t_done, t - 1)
                        dve.scalar_tensor_tensor(h[b], x[b][:], r, gn[:], ALU.mult, ALU.mult).then_inc(h_ready, 1)
                    else:
                        dve.wait_ge(hi_done, t + 1)
                        dve.tensor_tensor(hT_lo[:, :, tok(t)], turned, hT_hi[:, :, tok(t)].bitcast(F32), ALU.subtract).then_inc(lo_done, 1)

            @block.tensor
            def _(pe):
                def products(t, k):
                    for p, (a, b) in enumerate(((hT_lo, w_hi), (hT_hi, w_lo), (hT_hi, w_hi))):
                        for hf in range(2):
                            mm = weights_pass(pe, ps[t % NP][:, hf * HALF:(hf + 1) * HALF], a[:, k, tok(t)],
                                              b[:, k, hf * HALF:(hf + 1) * HALF], k == 0 and p == 0, k == KC - 1 and p == 2)
                    return mm

                def turn(t):
                    pe.wait_ge(h_ready, t + 1)
                    if t >= 1:
                        pe.wait_ge(lo_done, t)
                    for k in range(KC):
                        mm = pe.transpose(pt[:, k * P:(k + 1) * P], h[t % 2][:, k * P:(k + 1) * P], C["ident"][:])
                    mm.then_inc(t_done, 1)

                for k in range(KC):
                    pe.wait_ge(x_lo_done, k + 1)
                    pe.wait_ge(W.lo_done, U0 + k + 1)
                    for t in range(NP):
                        mm = products(t, k)
                        if k == KC - 1:
                            mm.then_inc(full, 1)
                for t in range(NP, NT):
                    pe.wait_ge(scaled, t - NP + 1)
                    for k in range(KC):
                        mm = products(t, k)
                    mm.then_inc(full, 1)
                    for n in TURNS[t]:
                        turn(n)


CONV, SILU, PLAIN = 14, 6, 4
N_FEAT = CONV + SILU + PLAIN
SMALL = 16


def layer2_projections(nc, C, W, U0, hT_hi, hT_lo, conv_par, w_small, feats, small_out):
    with ExitStack() as ctx:
        sb = lambda n, s, d=F32: ctx.enter_context(nc.sbuf_tensor(f"p2_{n}", s, d))
        sem = lambda n: ctx.enter_context(nc.semaphore(f"p2_{n}"))
        PADC = 3
        raw = [sb(f"raw{s}", [P, PADC + T]) for s in range(2)]
        acc = [sb(f"acc{s}", [P, T]) for s in range(2)]
        res = [sb(f"res{s}", [P, T]) for s in range(2)]
        par = sb("par", [P, CONV, 5])
        ws, ws_hi, ws_lo = sb("ws", [P, KC * SMALL]), sb("ws_hi", [P, KC * SMALL], F32R), sb("ws_lo", [P, KC * SMALL], F32R)
        G = [ctx.enter_context(nc.psum_tensor(f"p2_ps{s}", [P, T], F32)) for s in range(2)]
        S = ctx.enter_context(nc.psum_tensor("p2_small", [P, T], F32))
        small_T = sb("small_T", [SMALL, T])
        full, step, conv_out, pads = sem("full"), sem("step"), sem("conv_out"), sem("pads")
        evac = [sem(f"evac{s}") for s in range(2)]
        silu_done = [sem(f"silu_done{s}") for s in range(2)]
        stored = [sem(f"stored{s}") for s in range(2)]
        par_here, ws_hi_done, ws_lo_done, small_done, small_read = (sem(n) for n in (
            "par_here", "ws_hi_done", "ws_lo_done", "small_done", "small_read"))

        def all_units(eng, body):
            for kind, first, n in (("conv", 0, CONV), ("silu", CONV, SILU), ("plain", CONV + SILU, PLAIN)):
                if kind == "plain":
                    for c in range(n):
                        body(kind, first + c, 0, 0)
                    continue
                with eng.Fori(0, n // 2) as i:
                    for s in range(2):
                        body(kind, first + s, 2, i)

        with nc.Block() as block:
            @block.sync
            def _(sp):
                sp.dma_start(par[:], conv_par).then_inc(par_here, 16)
                sp.dma_start(ws[:], w_small).then_inc(par_here, 16)

                def body(kind, c, k, i):
                    if c % 2 == 0:
                        W.load(sp, U0 + 2 + c, k, i)
                        W.load(sp, U0 + 3 + c, k, i)
                    sp.wait_ge(silu_done[c % 2], c // 2 + 1 + i * (k // 2))
                    sp.dma_start(feats[c + k * i], res[c % 2][:]).then_inc(stored[c % 2], 16)
                all_units(sp, body)
                for s in range(2):
                    sp.wait_ge(stored[s], 16 * (N_FEAT // 2))

            @block.scalar
            def _(act):
                act.wait_ge(par_here, 32)
                act.copy(ws_hi[:], ws[:]).then_inc(ws_hi_done, 1)
                W.split_hi(act, U0)
                W.split_hi(act, U0 + 1)

                def body(kind, c, k, i):
                    b, n = c % 2, c // 2 + (k // 2) * i
                    act.wait_ge(full, c + 1 + k * i)
                    if kind == "conv":
                        act.wait_ge(conv_out, c - c % 2 + k * i)
                        act.copy(raw[b][:, PADC:], G[b][:]).then_inc(evac[b], 1)
                        W.split_hi(act, U0 + 2 + c, k, i)
                        act.wait_ge(conv_out, c + 1 + k * i)
                        act.wait_ge(stored[b], 16 * n)
                        act.activation(res[b][:], acc[b][:], ACT.Silu).then_inc(silu_done[b], 1)
                    else:
                        act.wait_ge(stored[b], 16 * n)
                        if kind == "silu":
                            act.activation(res[b][:], G[b][:], ACT.Silu).then_inc(silu_done[b], 1)
                        else:
                            scale = 64 ** -0.5 if c < CONV + SILU + 2 else 1.0
                            act.mul(res[b][:], G[b][:], scale).then_inc(silu_done[b], 1)
                        if c + 2 < N_FEAT or k:
                            W.split_hi(act, U0 + 2 + c, k, i)
                all_units(act, body)

            @block.vector
            def _(dve):
                for s in range(2):
                    dve.memset(raw[s][:, 0:PADC], 0.0).then_inc(pads, 1)
                dve.wait_ge(ws_hi_done, 1)
                dve.tensor_tensor(ws_lo[:], ws[:], ws_hi[:].bitcast(F32), ALU.subtract).then_inc(ws_lo_done, 1)
                W.split_lo(dve, U0)
                W.split_lo(dve, U0 + 1)
                dve.wait_ge(par_here, 32)
                dve.wait_ge(pads, 2)
                dve.wait_ge(small_done, 1)
                dve.tensor_copy(small_T[:], S[0:SMALL, :]).then_inc(small_read, 1)

                def body(kind, c, k, i):
                    b = c % 2
                    if kind == "conv":
                        n = c + k * i
                        W.split_lo(dve, U0 + 2 + c, k, i)
                        dve.wait_ge(evac[b], c // 2 + 1 + (k // 2) * i)
                        dve.wait_ge(silu_done[b], c // 2 + (k // 2) * i)
                        dve.tensor_scalar(acc[b][:], raw[b][:, 3:], par[:, bass.ds(n, 1), 3], par[:, bass.ds(n, 1), 4],
                                          ALU.mult, ALU.add).then_inc(step, 1)
                        for t in (2, 1, 0):
                            dve.wait_ge(step, 3 * n + 3 - t)
                            dve.scalar_tensor_tensor(acc[b][:], raw[b][:, t:t + T], par[:, bass.ds(n, 1), t], acc[b][:],
                                                     ALU.mult, ALU.add).then_inc(step if t else conv_out, 1)
                    elif c + 2 < N_FEAT or k:
                        W.split_lo(dve, U0 + 2 + c, k, i)
                all_units(dve, body)
                dve.wait_ge(small_done, 2)
                dve.tensor_copy(small_out[:].rearrange("p t c -> p (t c)"), S[:, 0:NT * SMALL]).then_inc(small_read, 1)

            @block.tensor
            def _(pe):
                pe.wait_ge(ws_lo_done, 1)
                for k in range(KC):
                    for p, (a, b) in enumerate(((ws_lo, hT_hi), (ws_hi, hT_lo), (ws_hi, hT_hi))):
                        for hf in range(2):
                            mm = weights_pass(pe, S[0:SMALL, hf * HALF:(hf + 1) * HALF], a[:, k * SMALL:(k + 1) * SMALL],
                                              b[:, k, hf * HALF:(hf + 1) * HALF], k == 0 and p == 0, k == KC - 1 and p == 2)
                mm.then_inc(small_done, 1)

                def body(kind, c, k, i):
                    b = c % 2
                    pe.wait_ge(W.lo_done, U0 + c + 1 + k * i)
                    if kind == "conv":
                        pe.wait_ge(evac[b], c // 2 + (k // 2) * i)
                    else:
                        pe.wait_ge(silu_done[b], c // 2 + (k // 2) * i)
                    for kc in range(KC):
                        for p, (a, r) in enumerate(((W.lo, hT_hi), (W.hi, hT_lo), (W.hi, hT_hi))):
                            for hf in range(2):
                                mm = weights_pass(pe, G[b][:, hf * HALF:(hf + 1) * HALF], a[b][:, kc * P:(kc + 1) * P],
                                                  r[:, kc, hf * HALF:(hf + 1) * HALF], kc == 0 and p == 0, kc == KC - 1 and p == 2)
                    mm.then_inc(full, 1)
                all_units(pe, body)
                pe.wait_ge(small_read, 1)
                for t in range(NT):
                    mm = pe.transpose(S[:, t * SMALL:(t + 1) * SMALL], small_T[:, t * P:(t + 1) * P], C["ident"][0:SMALL, 0:SMALL])
                mm.then_inc(small_done, 1)


NH = 12
SH, GH, AH = 8, 4, 4
PDT, PEA, PED, PBE, PACS, PDA, PES, PET, PEND = 0, 8, 20, 32, 36, 48, 60, 62, 70
LEVELS = (2, 4, 8, 16, 32, 64)
NEG = -1.0e30
ROW = dict(bias=0, alog=12, sinks=24, dskip=28, ssd_norm=36, gdn_norm=548, qk_scale=612, end=620)


class Steps:

    def __init__(self, sem, names):
        self.sem, self.names, self.at = sem, names.split(), 0

    def open(self, eng):
        eng.sem_inc(self.sem, len(self.names))

    def done(self, name, ins):
        assert self.names[self.at % len(self.names)] == name, (name, self.names[self.at % len(self.names)])
        self.at += 1
        ins.then_inc(self.sem, 1)

    def wait(self, eng, name, i):
        eng.wait_ge(self.sem, len(self.names) * (i + 1) + self.names.index(name) + 1)

    def wait_last(self, eng, name, i):
        eng.wait_ge(self.sem, len(self.names) * i + self.names.index(name) + 1)


def layer2_decays(nc, C, small, rows, prm):
    with ExitStack() as ctx:
        sb = lambda n, s, d=F32: ctx.enter_context(nc.sbuf_tensor(f"dc_{n}", s, d))
        sem = lambda n: ctx.enter_context(nc.semaphore(f"dc_{n}"))
        x, t = sb("x", [P, NT, NH]), sb("t", [P, NT, NH])
        ea, eb, et = sb("ea", [P, NH]), sb("eb", [P, NT, GH]), sb("et", [P, NT, NH])
        dif, da = sb("dif", [P, NT, NH]), sb("da", [P, NT, NH])
        ps = [ctx.enter_context(nc.psum_tensor(f"dc_ps{s}", [P, NT, NH], F32)) for s in range(2)]
        v, a, m = sem("vector"), sem("scalar"), sem("tensor")
        over_tiles = lambda r: r.unsqueeze(1).to_broadcast([P, NT, NH])
        with nc.Block() as block:
            @block.vector
            def _(dve):
                dve.tensor_tensor(x[:], small[:, :, 0:NH], over_tiles(rows[:, ROW["bias"]:ROW["bias"] + NH]), ALU.add).then_inc(v, 1)
                dve.wait_ge(a, 3)
                dve.scalar_tensor_tensor(x[:], x[:], 0.0, t[:], ALU.max, ALU.add).then_inc(v, 1)
                dve.wait_ge(v, 2)
                dve.wait_ge(a, 5)
                dve.tensor_copy(prm[:, :, PDT:PDT + SH], x[:, :, 0:SH]).then_inc(v, 1)
                dve.scalar_tensor_tensor(da[:], x[:], -1.0, over_tiles(ea[:]), ALU.mult, ALU.mult).then_inc(v, 1)
                dve.tensor_scalar(eb[:], eb[:], 1.0, None, ALU.add).then_inc(v, 1)
                dve.wait_ge(v, 5)
                dve.reciprocal(prm[:, :, PBE:PBE + GH], eb[:]).then_inc(v, 1)
                dve.tensor_copy(prm[:, :, PDA:PDA + NH], da[:]).then_inc(v, 1)
                dve.wait_ge(m, 2)
                dve.tensor_copy(prm[:, :, PACS:PACS + NH], ps[0][:]).then_inc(v, 1)
                dve.wait_ge(v, 8)
                dve.tensor_tensor(dif[:], ps[1][:], prm[:, :, PACS:PACS + NH], ALU.subtract).then_inc(v, 1)
                dve.wait_ge(a, 8)
                dve.tensor_copy(prm[:, :, PET:PET + SH], et[:, :, 0:SH]).then_inc(v, 1)
                for h in range(2):
                    rng = slice(64 * h, 64 * h + 64)
                    dve.tensor_copy(prm[rng, :, PES:PES + 2], et[rng, :, SH + h:NH:2]).then_inc(v, 1)
                dve.wait_ge(v, 12)

            @block.scalar
            def _(act):
                act.add_instruction(mybir.InstLoadActFuncSet(name=nc.get_next_instruction_name(), act_func_set_id=EXP_LN_SET))
                act.wait_ge(v, 1)
                act.activation(t[:], x[:], ACT.Abs).then_inc(a, 1)
                act.wait_ge(a, 1)
                act.activation(t[:], t[:], ACT.Exp, scale=-1.0).then_inc(a, 1)
                act.wait_ge(a, 2)
                act.activation(t[:], t[:], ACT.Ln, bias=1.0).then_inc(a, 1)
                act.activation(ea[:], rows[:, ROW["alog"]:ROW["alog"] + NH], ACT.Exp).then_inc(a, 1)
                act.activation(eb[:], small[:, :, NH:SMALL], ACT.Exp, scale=-1.0).then_inc(a, 1)
                act.wait_ge(v, 8)
                act.activation(prm[:, :, PEA:PEA + NH], prm[:, :, PACS:PACS + NH], ACT.Exp).then_inc(a, 1)
                act.wait_ge(v, 9)
                act.activation(et[:], ps[1][:], ACT.Exp).then_inc(a, 1)
                act.activation(prm[:, :, PED:PED + NH], dif[:], ACT.Exp).then_inc(a, 1)
                act.wait_ge(a, 8)

            @block.tensor
            def _(pe):
                pe.wait_ge(v, 4)
                for n, c in enumerate(("upto", "one")):
                    pe.matmul(ps[n][:].rearrange("p t h -> p (t h)"), C[c][:], da[:].rearrange("p t h -> p (t h)"),
                              start=True, stop=True).then_inc(m, 1)


def layer2_mixers(nc, C, feats, rows, prm, masks, attn_bias, mixT):
    with ExitStack() as ctx:
        sb = lambda n, s, d=F32: ctx.enter_context(nc.sbuf_tensor(f"m2_{n}", s, d))
        sem = lambda n: ctx.enter_context(nc.semaphore(f"m2_{n}"))
        F = sb("feat", [P, N_FEAT, P])
        XS0, B0, C0, GQ0, GV0, Z0, GZ0, AQ0, AK0, AV0 = 0, 4, 6, 8, 12, 14, 18, 20, 22, 23
        BC, AQK = sb("bc", [P, 4, P]), sb("aqk", [P, 3, P])
        XS, QK, VB, Z, GA = sb("xs", [P, 512]), sb("qk", [P, 512]), sb("vb", [P, 512]), sb("z", [P, 512]), sb("ga", [P, 384])
        PT = sb("par", [P, PEND])
        DEC = sb("dec", [P, NH, P])
        SQ, ss, rr = sb("sq", [P, 512]), sb("ss", [P, 8]), sb("rr", [P, 8])
        NQK = sb("nqk", [P, 512])
        KB, QG, KBG, KD, VBT = (sb(n, [P, 256]) for n in ("kb", "qg", "kbg", "kd", "vbt"))
        GZN, XD = sb("gzn", [P, 256]), sb("xd", [P, 512])
        XDT, XDE = sb("xdt", [P, 512]), sb("xde", [P, 512])
        KT, QT = sb("kt", [P, 4, P]), sb("qt", [P, 4, P])
        NTR, QKD = sb("ntr", [P, GH, P]), sb("qkd", [P, GH, P])
        NM = sb("nm", [P, len(LEVELS), GH, P])
        VT, V, T1 = sb("vt", [P, GH, P]), sb("v", [P, GH, P]), sb("t1", [P, GH, P])
        SD = sb("sd", [P, SH, P])
        Y = sb("y", [P, 512])
        yss, yrr, oss, orr = sb("yss", [P, 2]), sb("yrr", [P, 2]), sb("oss", [P, 4]), sb("orr", [P, 4])
        ST, S = sb("ssd_state", [P, 512]), sb("gdn_state", [P, 2, P])
        WT, VN, SQO, OG = sb("wt", [P, 2, P]), sb("vn", [P, 256]), sb("sqo", [P, 256]), sb("og", [P, 256])
        SS, bias = sb("scores", [P, AH, 256]), sb("bias", [P, AH, 256])
        mx, ngm, sdif, sums, es, den, rden = (sb(n, [P, AH]) for n in ("mx", "ngm", "sdif", "sums", "es", "den", "rden"))
        PTR = sb("ptr", [P, 2 * AH, P])
        KP, VP = sb("k_prev", [P, P]), sb("v_prev", [P, P])
        M = sb("mix", [P, D])
        MSK = sb("masks", [P, 2 + len(LEVELS), P])
        BR = sb("bias_rest", [P, AH, 256])
        zero = sb("zero", [P, 1])
        PS = ctx.enter_context(nc.psum_tensor("m2_ps", [P, 8, 512], F32))
        bank = lambda b, n=1: PS[:, b:b + n, :].rearrange("p b c -> p (b c)")
        heads = lambda ap, h: ap.rearrange("p (h c) -> p h c", h=h)
        per = lambda ap, h, n: ap.unsqueeze(2).to_broadcast([P, h, n])
        over = lambda ap, h: ap.unsqueeze(1).to_broadcast([P, h, ap.shape[-1]])
        row = lambda n, w: rows[:, ROW[n]:ROW[n] + w]
        half = lambda h: slice(64 * (h % 2), 64 * (h % 2) + 64)

        tens = Steps(sem("tensor"), "tr0 tr1 tr2 tr3 tr4 lb sc swas gtk gtq qk v1t T2 yo X2 T4 y stn X4 ptr T8 X8 att T16 X16 "
                                    "T32 X32 T64 X64 wt vn o ds mtr")
        scal = Steps(sem("scalar"), "xs qk vb z ga sq lnr expr L e0 e1 e2 e3 es kt qt v1 T2 T4 T8 pt T16 yq0 yq1 yln yexp T32 T64 "
                                    "wt vn osq oln oexp mt")
        vect = Steps(sem("vector"), "dsub dmask ss ssc nqk kb qg swab mx mx2 ngm sdif nt qkd m1 vt1 xdt xdec sd0 sd1 V2 VT2 "
                                    "yo y V4 VT4 yx yz st1 st2 den rden V8 VT8 ysc V16 VT16 att V32 VT32 ym0 ym1 VT64 s0 s1 s2 s3 oss osc og ogz")
        pool = Steps(sem("gpsimd"), "par keep0 keep1 kbg kd vb gzn xd nm0 nm1 nm2 nm3 nm4 nm5 kprev vprev bias")
        f_here, c_here, z_init = sem("feats_here"), sem("consts_here"), sem("zeroed")

        with nc.Block() as block:
            @block.sync
            def _(sp):
                sp.dma_start(MSK[:], masks).then_inc(c_here, 16)
                sp.dma_start(bias[:], attn_bias[0]).then_inc(c_here, 16)
                sp.dma_start(BR[:], attn_bias[1]).then_inc(c_here, 16)
                with sp.Fori(0, NT) as i:
                    tens.wait_last(sp, "tr4", i)
                    pool.wait_last(sp, "keep1", i)
                    sp.dma_start(F[:], feats[:, :, bass.ds(i * P, P)].rearrange("c p t -> p c t")).then_inc(f_here, 16)

            @block.gpsimd
            def _(g):
                pool.open(g)
                g.memset(KP[:], 0.0).then_inc(z_init, 1)
                g.memset(VP[:], 0.0).then_inc(z_init, 1)
                g.memset(zero[:], 0.0).then_inc(z_init, 1)
                g.wait_ge(c_here, 48)
                g.wait_ge(z_init, 5)
                with g.Fori(0, NT) as i:
                    vect.wait_last(g, "s3", i)
                    tens.wait_last(g, "lb", i)
                    pool.done("par", g.tensor_copy(PT[:], prm[:, bass.ds(i, 1), :].rearrange("p a c -> p (a c)")))
                    g.wait_ge(f_here, 16 * i + 16)
                    tens.wait_last(g, "stn", i)
                    tens.wait_last(g, "swas", i)
                    pool.done("keep0", copy(g, BC[:], F[:, B0:B0 + 4, :], zero))
                    pool.wait_last(g, "kprev", i)
                    pool.done("keep1", copy(g, AQK[:], F[:, AQ0:AQ0 + 3, :], zero))
                    vect.wait(g, "kb", i)
                    tens.wait_last(g, "wt", i)
                    pool.done("kbg", g.tensor_tensor(heads(KBG[:], GH), heads(KB[:], GH), per(PT[:, PEA + SH:PEA + NH], GH, 64), ALU.mult))
                    tens.wait_last(g, "ds", i)
                    pool.done("kd", g.tensor_tensor(heads(KD[:], GH), heads(NQK[:, 256:], GH), per(PT[:, PED + SH:PED + NH], GH, 64), ALU.mult))
                    scal.wait(g, "vb", i)
                    tens.wait_last(g, "vn", i)
                    pool.done("vb", g.tensor_tensor(heads(VBT[:], GH), heads(VB[:, 0:256], GH), per(PT[:, PBE:PBE + GH], GH, 64), ALU.mult))
                    scal.wait(g, "ga", i)
                    vect.wait_last(g, "ogz", i)
                    pool.done("gzn", g.tensor_tensor(heads(GZN[:], GH), heads(GA[:, 0:256], GH), over(row("gdn_norm", 64), GH), ALU.mult))
                    scal.wait(g, "xs", i)
                    vect.wait_last(g, "yx", i)
                    pool.done("xd", g.tensor_tensor(heads(XD[:], SH), heads(XS[:], SH), per(row("dskip", SH), SH, 64), ALU.mult))
                    vect.wait(g, "nt", i)
                    tens.wait_last(g, "T64", i)
                    for n in range(len(LEVELS)):
                        pool.done(f"nm{n}", g.tensor_tensor(NM[:, n], NTR[:], over(MSK[:, 2 + n, :], GH), ALU.mult))
                    tens.wait(g, "swas", i)
                    pool.wait(g, "keep1", i)
                    pool.done("kprev", copy(g, KP[:], AQK[:, 2, :], zero))
                    tens.wait(g, "att", i)
                    pool.done("vprev", copy(g, VP[:], GA[:, 256:384], zero))
                    vect.wait(g, "swab", i)
                    pool.done("bias", copy(g, bias[:], BR[:], zero))

            @block.scalar
            def _(a):
                scal.open(a)
                a.add_instruction(mybir.InstLoadActFuncSet(name=nc.get_next_instruction_name(), act_func_set_id=EXP_LN_SET))
                with a.Fori(0, NT) as i:
                    def inverse_root(tag, out, src):
                        scal.done(tag + "ln" if tag != "r" else "lnr", a.activation(out, src, ACT.Ln))
                        scal.wait(a, tag + "ln" if tag != "r" else "lnr", i)
                        scal.done(tag + "exp" if tag != "r" else "expr", a.activation(out, out, ACT.Exp, scale=-0.5))

                    tens.wait(a, "tr0", i)
                    pool.wait_last(a, "xd", i)
                    vect.wait_last(a, "xdt", i)
                    scal.done("xs", a.copy(XS[:], bank(0)))
                    tens.wait(a, "tr1", i)
                    vect.wait_last(a, "nqk", i)
                    scal.done("qk", a.copy(QK[:], bank(1)))
                    tens.wait(a, "tr2", i)
                    pool.wait_last(a, "vb", i)
                    tens.wait_last(a, "stn", i)
                    scal.done("vb", a.copy(VB[:], bank(2)))
                    tens.wait(a, "tr3", i)
                    vect.wait_last(a, "yz", i)
                    scal.done("z", a.copy(Z[:], bank(3)))
                    tens.wait(a, "tr4", i)
                    pool.wait_last(a, "vprev", i)
                    scal.done("ga", a.copy(GA[:], PS[:, 4, 0:384]))
                    scal.wait(a, "qk", i)
                    scal.done("sq", a.activation(SQ[:], QK[:], ACT.Square))
                    vect.wait(a, "ssc", i)
                    inverse_root("r", rr[:], ss[:])
                    vect.wait(a, "dmask", i)
                    scal.done("L", a.activation(DEC[:], DEC[:], ACT.Exp))
                    vect.wait(a, "sdif", i)
                    for h in range(AH):
                        scal.done(f"e{h}", a.activation(SS[:, h], SS[:, h], ACT.Exp, bias=ngm[:, h:h + 1], accum_out=sums[:, h:h + 1]))
                    scal.done("es", a.activation(es[:], sdif[:], ACT.Exp))
                    tens.wait(a, "gtk", i)
                    tens.wait_last(a, "qk", i)
                    scal.done("kt", a.copy(KT[:].rearrange("p n t -> p (n t)"), bank(5)))
                    tens.wait(a, "gtq", i)
                    tens.wait_last(a, "o", i)
                    scal.done("qt", a.copy(QT[:].rearrange("p n t -> p (n t)"), bank(6)))
                    tens.wait(a, "v1t", i)
                    scal.done("v1", a.copy(V[:].rearrange("p h t -> p (h t)"), bank(7)))

                    def product(b):
                        tens.wait(a, f"T{b}", i)
                        tens.wait_last(a, "X64", i) if b == 2 else tens.wait(a, f"X{b // 2}", i)
                        scal.done(f"T{b}", a.copy(T1[:].rearrange("p h t -> p (h t)"), bank(5)))
                    product(2)
                    product(4)
                    product(8)
                    tens.wait(a, "ptr", i)
                    tens.wait_last(a, "att", i)
                    scal.done("pt", a.copy(PTR[:].rearrange("p n t -> p (n t)"), bank(1, 2)))
                    product(16)
                    vect.wait(a, "yz", i)
                    for g in range(2):
                        scal.done(f"yq{g}", a.activation(SQ[:, 256 * g:256 * g + 256], Y[:, 256 * g:256 * g + 256], ACT.Square,
                                                         accum_out=yss[:, g:g + 1]))
                    vect.wait(a, "ysc", i)
                    inverse_root("y", yrr[:], yss[:])
                    product(32)
                    product(64)
                    tens.wait(a, "wt", i)
                    scal.done("wt", a.mul(WT[:].rearrange("p n t -> p (n t)"), PS[:, 5, 0:256], -1.0))
                    tens.wait(a, "vn", i)
                    scal.done("vn", a.copy(VN[:], PS[:, 2, 0:256]))
                    tens.wait(a, "o", i)
                    scal.done("osq", a.activation(SQO[:], PS[:, 6, 0:256], ACT.Square))
                    vect.wait(a, "osc", i)
                    inverse_root("o", orr[:], oss[:])
                    tens.wait(a, "mtr", i)
                    scal.done("mt", a.copy(mixT[:, :, bass.ds(i * P, P)], bank(3, 2).rearrange("p (c t) -> p c t", c=KC)))

            @block.vector
            def _(v):
                vect.open(v)
                v.memset(ST[:], 0.0).then_inc(z_init, 1)
                v.memset(S[:], 0.0).then_inc(z_init, 1)
                v.wait_ge(z_init, 5)
                v.wait_ge(c_here, 48)
                with v.Fori(0, NT) as i:
                    tt = v.tensor_tensor
                    tens.wait(v, "lb", i)
                    pool.wait(v, "par", i)
                    vect.wait_last(v, "sd1", i)
                    vect.done("dsub", tt(DEC[:], bank(5, 3).rearrange("p (h t) -> p h t", h=NH), per(PT[:, PACS:PACS + NH], NH, P), ALU.subtract))
                    vect.wait(v, "dsub", i)
                    vect.done("dmask", v.scalar_tensor_tensor(DEC[:], DEC[:], 0.0, over(MSK[:, 0, :], NH), ALU.min, ALU.add))
                    scal.wait(v, "sq", i)
                    vect.done("ss", v.tensor_reduce(ss[:], heads(SQ[:], 8), AX, ALU.add))
                    vect.wait(v, "ss", i)
                    vect.done("ssc", v.scalar_tensor_tensor(ss[:], ss[:], EPS, row("qk_scale", 8), ALU.add, ALU.mult))
                    scal.wait(v, "expr", i)
                    vect.done("nqk", tt(heads(NQK[:], 8), heads(QK[:], 8), per(rr[:], 8, 64), ALU.mult))
                    vect.wait(v, "nqk", i)
                    vect.done("kb", tt(heads(KB[:], GH), heads(NQK[:, 256:], GH), per(PT[:, PBE:PBE + GH], GH, 64), ALU.mult))
                    vect.done("qg", tt(heads(QG[:], GH), heads(NQK[:, 0:256], GH), per(PT[:, PEA + SH:PEA + NH], GH, 64), ALU.mult))
                    tens.wait(v, "swas", i)
                    vect.done("swab", tt(SS[:].rearrange("p h k -> p (h k)"), bank(1, 2), bias[:].rearrange("p h k -> p (h k)"), ALU.add))
                    vect.wait(v, "swab", i)
                    vect.done("mx", v.tensor_reduce(mx[:], SS[:], AX, ALU.max))
                    vect.wait(v, "mx", i)
                    vect.done("mx2", tt(mx[:], mx[:], row("sinks", AH), ALU.max))
                    vect.wait(v, "mx2", i)
                    vect.done("ngm", v.tensor_scalar(ngm[:], mx[:], -1.0, None, ALU.mult))
                    vect.done("sdif", tt(sdif[:], row("sinks", AH), mx[:], ALU.subtract))
                    tens.wait(v, "qk", i)
                    scal.wait(v, "L", i)
                    by_parity = lambda ap: ap.rearrange("p (n b) t -> p b n t", b=2)
                    for n, (name, out) in enumerate((("nt", NTR), ("qkd", QKD))):
                        vect.done(name, tt(by_parity(out[:]), PS[:, 3:5, 256 * n:256 * n + 256].rearrange("p b (n t) -> p b n t", n=2),
                                           by_parity(DEC[:, SH:NH]), ALU.mult))
                    vect.wait(v, "nt", i)
                    vect.done("m1", tt(VT[:], NTR[:], over(MSK[:, 1, :], GH), ALU.mult))
                    vect.wait(v, "m1", i)
                    vect.done("vt1", tt(VT[:], VT[:], over(C["ident"][:], GH), ALU.add))
                    vect.done("xdt", tt(heads(XDT[:], SH), heads(XS[:], SH), per(PT[:, PDT:PDT + SH], SH, 64), ALU.mult))
                    vect.wait(v, "xdt", i)
                    vect.done("xdec", tt(heads(XDE[:], SH), heads(XDT[:], SH), per(PT[:, PED:PED + SH], SH, 64), ALU.mult))
                    for g in range(2):
                        vect.done(f"sd{g}", tt(SD[:, 4 * g:4 * g + 4], DEC[:, 4 * g:4 * g + 4],
                                               over(PS[:, 0, P * g:P * g + P], 4), ALU.mult))

                    def level(b):
                        tens.wait(v, f"X{b}", i)
                        if b < 64:
                            scal.wait(v, "v1", i)
                            vect.done(f"V{b}", tt(V[:].rearrange("p h t -> p (h t)"), V[:].rearrange("p h t -> p (h t)"), bank(6), ALU.subtract))
                        vect.done(f"VT{b}", tt(VT[:].rearrange("p h t -> p (h t)"), VT[:].rearrange("p h t -> p (h t)"), bank(7), ALU.subtract))

                    level(2)
                    tens.wait(v, "yo", i)
                    vect.done("yo", tt(heads(Y[:], SH), heads(bank(4), SH), per(PT[:, PEA:PEA + SH], SH, 64), ALU.mult))
                    tens.wait(v, "y", i)
                    vect.wait(v, "yo", i)
                    vect.done("y", tt(Y[:], Y[:], bank(3), ALU.add))
                    level(4)
                    pool.wait(v, "xd", i)
                    vect.wait(v, "y", i)
                    vect.done("yx", tt(Y[:], Y[:], XD[:], ALU.add))
                    vect.wait(v, "yx", i)
                    vect.done("yz", tt(Y[:], Y[:], Z[:], ALU.mult))
                    vect.done("st1", tt(heads(ST[:], SH), heads(ST[:], SH), per(PT[:, PET:PET + SH], SH, 64), ALU.mult))
                    vect.wait(v, "st1", i)
                    tens.wait(v, "stn", i)
                    vect.done("st2", tt(ST[:], ST[:], bank(0), ALU.add))
                    scal.wait(v, "es", i)
                    vect.done("den", tt(den[:], sums[:], es[:], ALU.add))
                    vect.wait(v, "den", i)
                    vect.done("rden", v.reciprocal(rden[:], den[:]))
                    level(8)
                    scal.wait(v, "yq1", i)
                    vect.done("ysc", v.tensor_scalar(yss[:], yss[:], 1.0 / 256, EPS, ALU.mult, ALU.add))
                    level(16)
                    tens.wait(v, "att", i)
                    tens.wait_last(v, "mtr", i)
                    vect.done("att", tt(heads(M[:, 0:256], AH), heads(PS[:, 1, 0:256], AH), per(rden[:], AH, 64), ALU.mult))
                    level(32)
                    scal.wait(v, "yexp", i)
                    for g in range(2):
                        c = slice(256 * g, 256 * g + 256)
                        vect.done(f"ym{g}", v.scalar_tensor_tensor(M[:, 256 + 256 * g:512 + 256 * g], Y[:, c], yrr[:, g:g + 1],
                                                                   row("ssd_norm", 512)[:, c], ALU.mult, ALU.mult))
                    level(64)
                    tens.wait(v, "ds", i)
                    for h in range(GH):
                        n, r = h // 2, half(h)
                        vect.done(f"s{h}", v.scalar_tensor_tensor(S[r, n, r], S[r, n, r], PT[r, PES + n:PES + n + 1],
                                                                  PS[r, 7, 64 * n:64 * n + 64], ALU.mult, ALU.add))
                    scal.wait(v, "osq", i)
                    vect.done("oss", v.tensor_reduce(oss[:], heads(SQO[:], GH), AX, ALU.add))
                    vect.wait(v, "oss", i)
                    vect.done("osc", v.tensor_scalar(oss[:], oss[:], 1.0 / 64, EPS, ALU.mult, ALU.add))
                    scal.wait(v, "oexp", i)
                    vect.done("og", tt(heads(OG[:], GH), heads(PS[:, 6, 0:256], GH), per(orr[:], GH, 64), ALU.mult))
                    vect.wait(v, "og", i)
                    pool.wait(v, "gzn", i)
                    vect.done("ogz", tt(M[:, 768:1024], OG[:], GZN[:], ALU.mult))

            @block.tensor
            def _(pe):
                tens.open(pe)
                with pe.Fori(0, NT) as i:
                    def turn(name, b, parts):
                        for n, part in enumerate(parts):
                            mm = pe.transpose(PS[:, b + n // 4, (n % 4) * P:(n % 4) * P + P], part, C["ident"][:])
                        tens.done(name, mm)

                    def mm(out, lhs, rhs, start=True, stop=True):
                        return pe.matmul(out, lhs, rhs, start=start, stop=stop, skip_group_check=True)

                    pe.wait_ge(f_here, 16 * i + 16)
                    vect.wait_last(pe, "st2", i)
                    turn("tr0", 0, [F[:, c] for c in range(XS0, XS0 + 4)])
                    vect.wait_last(pe, "att", i)
                    turn("tr1", 1, [F[:, c] for c in range(GQ0, GQ0 + 4)])
                    scal.wait_last(pe, "vn", i)
                    turn("tr2", 2, [F[:, c] for c in (GV0, GV0 + 1, B0, B0 + 1)])
                    scal.wait_last(pe, "mt", i)
                    turn("tr3", 3, [F[:, c] for c in range(Z0, Z0 + 4)])
                    turn("tr4", 4, [F[:, c] for c in (GZ0, GZ0 + 1, AV0)])
                    pool.wait(pe, "par", i)
                    vect.wait_last(pe, "og", i)
                    for h in range(NH):
                        x = mm(PS[:, 5 + h // 4, (h % 4) * P:(h % 4) * P + P], PT[:, PDA + h:PDA + h + 1].to_broadcast([P, P]), C["upto"][:])
                    tens.done("lb", x)
                    pool.wait(pe, "keep0", i)
                    scal.wait(pe, "xs", i)
                    for g in range(2):
                        x = mm(PS[:, 0, g * P:(g + 1) * P], BC[:, g], BC[:, 2 + g])
                    tens.done("sc", x)
                    pool.wait(pe, "keep1", i)
                    pool.wait_last(pe, "kprev", i)
                    pe.wait_ge(z_init, 5)
                    scal.wait(pe, "vb", i)
                    for h in range(AH):
                        kv = slice(64 * (h // 2), 64 * (h // 2) + 64)
                        for n, keys in enumerate((KP[kv, :], AQK[kv, 2, :])):
                            x = mm(PS[:, 1 + h // 2, (h % 2) * 256 + n * P:(h % 2) * 256 + n * P + P], AQK[kv, h % 2, :], keys)
                    tens.done("swas", x)
                    vect.wait(pe, "qg", i)
                    turn("gtk", 5, [NQK[:, 256:384], NQK[:, 384:512], KB[:, 0:128], KB[:, 128:256]])
                    turn("gtq", 6, [NQK[:, 0:128], NQK[:, 128:256], QG[:, 0:128], QG[:, 128:256]])
                    scal.wait(pe, "kt", i)
                    scal.wait(pe, "z", i)
                    for h in range(GH):
                        mm(PS[:, 3 + h % 2, (h // 2) * P:(h // 2 + 1) * P], KT[half(h), h // 2], KT[half(h), 2 + h // 2])
                    scal.wait(pe, "qt", i)
                    for h in range(GH):
                        x = mm(PS[:, 3 + h % 2, (2 + h // 2) * P:(3 + h // 2) * P], KT[half(h), h // 2], QT[half(h), h // 2])
                    tens.done("qk", x)
                    vect.wait(pe, "vt1", i)
                    turn("v1t", 7, [VT[:, h] for h in range(GH)])

                    def level_t(b):
                        scal.wait(pe, "v1", i)
                        pool.wait(pe, f"nm{LEVELS.index(b)}", i)
                        if b > 2:
                            vect.wait(pe, f"VT{b // 2}", i)
                        for h in range(GH):
                            x = mm(PS[:, 5, h * P:(h + 1) * P], NM[:, LEVELS.index(b), h], V[:, h])
                        tens.done(f"T{b}", x)

                    def level_x(b):
                        scal.wait(pe, f"T{b}", i)
                        for h in range(GH):
                            if b < 64:
                                mm(PS[:, 6, h * P:(h + 1) * P], VT[:, h], T1[:, h])
                            x = mm(PS[:, 7, h * P:(h + 1) * P], T1[:, h], VT[:, h])
                        tens.done(f"X{b}", x)

                    level_t(2)
                    vect.wait(pe, "qkd", i)
                    vect.wait_last(pe, "st2", i)
                    for g in range(2):
                        x = mm(PS[:, 4, 256 * g:256 * g + 256], BC[:, 2 + g], ST[:, 256 * g:256 * g + 256])
                    tens.done("yo", x)
                    level_x(2)
                    level_t(4)
                    vect.wait(pe, "sd1", i)
                    for h in range(SH):
                        x = mm(PS[:, 3, 64 * h:64 * h + 64], SD[:, h], XDT[:, 64 * h:64 * h + 64])
                    tens.done("y", x)
                    for g in range(2):
                        x = mm(PS[:, 0, 256 * g:256 * g + 256], VB[:, 256 + P * g:384 + P * g], XDE[:, 256 * g:256 * g + 256])
                    tens.done("stn", x)
                    level_x(4)
                    scal.wait(pe, "es", i)
                    turn("ptr", 1, [SS[:, h, n * P:(n + 1) * P] for h in range(AH) for n in range(2)])
                    level_t(8)
                    level_x(8)
                    scal.wait(pe, "pt", i)
                    scal.wait(pe, "ga", i)
                    pool.wait_last(pe, "vprev", i)
                    for h in range(AH):
                        kv = 64 * (h // 2)
                        mm(PS[:, 1, 64 * h:64 * h + 64], PTR[:, 2 * h], VP[:, kv:kv + 64], True, False)
                        x = mm(PS[:, 1, 64 * h:64 * h + 64], PTR[:, 2 * h + 1], GA[:, 256 + kv:320 + kv], False, True)
                    tens.done("att", x)
                    for b in (16, 32, 64):
                        level_t(b)
                        level_x(b)
                    vect.wait(pe, "VT64", i)
                    pool.wait(pe, "vb", i)
                    for h in range(GH):
                        x = mm(PS[half(h), 5, (h // 2) * P:(h // 2) * P + P], KBG[:, 64 * h:64 * h + 64], VT[:, h])
                    tens.done("wt", x)
                    scal.wait(pe, "wt", i)
                    vect.wait_last(pe, "s3", i)
                    for n in range(2):
                        c = slice(P * n, P * n + P)
                        mm(PS[:, 2, c], WT[:, n], S[:, n], True, False)
                        for h in (2 * n, 2 * n + 1):
                            x = mm(PS[:, 2, 64 * h:64 * h + 64], VT[:, h], VBT[:, 64 * h:64 * h + 64], False, True)
                    tens.done("vn", x)
                    scal.wait(pe, "vn", i)
                    for n in range(2):
                        mm(PS[:, 6, P * n:P * n + P], QT[:, 2 + n], S[:, n], True, False)
                        for h in (2 * n, 2 * n + 1):
                            x = mm(PS[:, 6, 64 * h:64 * h + 64], QKD[:, h], VN[:, 64 * h:64 * h + 64], False, True)
                    tens.done("o", x)
                    for h in range(GH):
                        c = slice(64 * h, 64 * h + 64)
                        x = mm(PS[half(h), 7, (h // 2) * 64:(h // 2) * 64 + 64], KD[:, c], VN[:, c])
                    tens.done("ds", x)
                    vect.wait(pe, "ogz", i)
                    turn("mtr", 3, [M[:, c * P:(c + 1) * P] for c in range(KC)])


def layer2_ffn(nc, W, U0, hT_hi, hT_lo, f, x_in, g_post, out):
    with ExitStack() as ctx:
        sb = lambda n, s, d=F32: ctx.enter_context(nc.sbuf_tensor(f"ff_{n}", s, d))
        sem = lambda n: ctx.enter_context(nc.semaphore(f"ff_{n}"))
        NCH = 22
        gate = [sb(f"gate{s}", [P, T]) for s in range(2)]
        act_v = [sb(f"act{s}", [P, T]) for s in range(2)]
        a_hi = [sb(f"a_hi{s}", [P, T], F32R) for s in range(2)]
        a_lo = [sb(f"a_lo{s}", [P, T], F32R) for s in range(2)]
        G = [ctx.enter_context(nc.psum_tensor(f"ff_g{s}", [P, T], F32)) for s in range(2)]
        O = [ctx.enter_context(nc.psum_tensor(f"ff_o{s}", [P, D], F32)) for s in range(2)]
        g_full, u_full, gated, hidden, a_hi_done, a_lo_done = (sem(n) for n in ("g_full", "u_full", "gated", "hidden", "a_hi_done", "a_lo_done"))
        o_full, added, zeroed = sem("o_full"), sem("added"), sem("zeroed")
        x, gain, st, junk = sb("x", [P, NT, D]), sb("gain", [P, D]), sb("stat", [P, NT, 4]), [sb(f"junk{s}", [P, D]) for s in range(2)]
        x_here, sq, ms, rt, rc, scaled, x_new, stored = (sem(n) for n in ("x_here", "sq", "ms", "rt", "rc", "scaled", "x_new", "stored"))
        x_t = x_in.rearrange("(t p) d -> t p d", p=P)
        out_t = out.rearrange("(t p) d -> t p d", p=P)
        gate_u = lambda c: 0 if c == 0 else 3 * c - 1
        up_u = lambda c: gate_u(c) + 1
        down_u = lambda c: 3 * c + 4 if c < NCH - 1 else 3 * NCH - 1

        def in_order(eng, first, chunk, last):
            first()
            with eng.Fori(0, (NCH - 2) // 2) as i:
                chunk(1, i)
                chunk(2, i)
            chunk(NCH - 1, 0)
            last()

        with nc.Block() as block:
            @block.sync
            def _(sp):
                def chunk(c, i):
                    for u in range(3):
                        if gate_u(c) + 2 + u + U0 < U0 + 3 * NCH:
                            W.load(sp, U0 + gate_u(c) + 2 + u, 6, i)
                def first():
                    W.load(sp, U0 + 2)
                    W.load(sp, U0 + 3)
                    sp.dma_start(gain[:], g_post.to_broadcast([P, D])).then_inc(x_here, 16)
                    for t in range(NT):
                        sp.dma_start(x[:, t, :], x_t[t]).then_inc(x_here, 16)

                def last():
                    for t in range(NT):
                        sp.wait_ge(x_new, t + 1)
                        sp.dma_start(out_t[t], x[:, t, :]).then_inc(stored, 16)
                    sp.wait_ge(stored, 16 * NT)

                in_order(sp, first, chunk, last)

            @block.gpsimd
            def _(pool):
                pool.wait_ge(x_here, 16 * (NT + 1))
                for t in range(NT):
                    pool.wait_ge(scaled, t + 1)
                    pool.tensor_tensor(x[:, t, :], x[:, t, :], f[:, t, :], ALU.add).then_inc(x_new, 1)

            @block.scalar
            def _(act):
                def split(u, i):
                    prev = u - 2
                    if prev == 0:
                        act.wait_ge(g_full, 1)
                    elif prev == 1:
                        act.wait_ge(u_full, 1)
                    else:
                        kind, c = (prev - 2) % 3, (prev - 2) // 3 + 1
                        if prev == 3 * NCH - 1:
                            return
                        if kind == 0:
                            act.wait_ge(g_full, c + 1 + 2 * i)
                        elif kind == 1:
                            act.wait_ge(u_full, c + 1 + 2 * i)
                        else:
                            act.wait_ge(o_full, NT * c + 2 * NT * i)
                    W.split_hi(act, U0 + u, 6, i)

                def gating(c, i):
                    b = c % 2
                    act.wait_ge(g_full, c + 1 + 2 * i)
                    if c >= 1:
                        act.wait_ge(hidden, c - 1 + 2 * i)
                    act.activation(gate[b][:], G[0][:], ACT.Silu).then_inc(gated, 1)

                def high(c, i):
                    b = c % 2
                    act.wait_ge(hidden, c + 1 + 2 * i)
                    if c >= 1:
                        act.wait_ge(o_full, NT * (c - 1) + 2 * NT * i)
                    act.copy(a_hi[b][:], act_v[b][:]).then_inc(a_hi_done, 1)

                def first():
                    W.split_hi(act, U0)
                    W.split_hi(act, U0 + 1)
                    gating(0, 0)
                    split(2, 0)
                    split(3, 0)
                    high(0, 0)

                def chunk(c, i):
                    g = gate_u(c)
                    gating(c, i)
                    split(g + 2, i)
                    if g + 3 < 3 * NCH:
                        split(g + 3, i)
                    high(c, i)
                    if c < NCH - 1:
                        split(g + 4, i)

                def last():
                    for t in range(NT):
                        act.wait_ge(added, NT * (NCH - 1) + t + 1)
                        act.activation(junk[t % 2][:], f[:, t, :], ACT.Square, accum_out=st[:, t, 0:1]).then_inc(sq, 1)
                        if t >= 1:
                            root(t - 1)
                    root(NT - 1)

                def root(t):
                    act.wait_ge(ms, t + 1)
                    act.activation(st[:, t, 2:3], st[:, t, 1:2], ACT.Sqrt).then_inc(rt, 1)

                in_order(act, first, chunk, last)

            @block.vector
            def _(dve):
                def split(u, i):
                    W.split_lo(dve, U0 + u, 6, i)

                def product(c, i):
                    b = c % 2
                    dve.wait_ge(gated, c + 1 + 2 * i)
                    dve.wait_ge(u_full, c + 1 + 2 * i)
                    if c >= 1:
                        dve.wait_ge(a_lo_done, c - 1 + 2 * i)
                    dve.tensor_tensor(act_v[b][:], G[1][:], gate[b][:], ALU.mult).then_inc(hidden, 1)

                def low(c, i):
                    b = c % 2
                    dve.wait_ge(a_hi_done, c + 1 + 2 * i)
                    dve.tensor_tensor(a_lo[b][:], act_v[b][:], a_hi[b][:].bitcast(F32), ALU.subtract).then_inc(a_lo_done, 1)

                def down(c, i, first, last):
                    for t in range(first, last):
                        dve.wait_ge(o_full, NT * c + t + 1 + 2 * NT * i)
                        dve.wait_ge(added, max(NT * (c - 1) + t + 1, 0) + 2 * NT * i)
                        dve.tensor_tensor(f[:, t, :], f[:, t, :], O[t % 2][:], ALU.add).then_inc(added, 1)

                def first():
                    split(0, 0)
                    split(1, 0)
                    dve.memset(f[:], 0.0).then_inc(zeroed, 1)
                    split(2, 0)
                    product(0, 0)
                    split(3, 0)
                    low(0, 0)
                    dve.wait_ge(zeroed, 1)

                def chunk(c, i):
                    g = gate_u(c)
                    if g + 2 < 3 * NCH:
                        split(g + 2, i)
                    product(c, i)
                    down(c - 1, i, 0, 2)
                    if g + 3 < 3 * NCH:
                        split(g + 3, i)
                    down(c - 1, i, 2, 4)
                    low(c, i)
                    down(c - 1, i, 4, NT)
                    if c < NCH - 1:
                        split(g + 4, i)

                def last():
                    dve.wait_ge(x_here, 16 * (NT + 1))
                    for t in range(NT + 2):
                        if t < NT:
                            down(NCH - 1, 0, t, t + 1)
                        if 1 <= t <= NT:
                            dve.wait_ge(sq, t)
                            dve.tensor_scalar(st[:, t - 1, 1:2], st[:, t - 1, 0:1], 1.0 / D, EPS, ALU.mult, ALU.add).then_inc(ms, 1)
                        if t >= 2:
                            n = t - 2
                            dve.wait_ge(rt, n + 1)
                            dve.reciprocal(st[:, n, 3:4], st[:, n, 2:3]).then_inc(rc, 1)
                            dve.wait_ge(rc, n + 1)
                            dve.scalar_tensor_tensor(f[:, n, :], f[:, n, :], st[:, n, 3:4], gain[:], ALU.mult, ALU.mult).then_inc(scaled, 1)

                in_order(dve, first, chunk, last)

            @block.tensor
            def _(pe):
                def unit(u, i, g, free, full):
                    pe.wait_ge(W.lo_done, U0 + u + 1 + 6 * i)
                    free()
                    for kc in range(KC):
                        for p, (a, r) in enumerate(((W.lo, hT_hi), (W.hi, hT_lo), (W.hi, hT_hi))):
                            for hf in range(2):
                                mm = weights_pass(pe, g[:, hf * HALF:(hf + 1) * HALF], a[u % 2][:, kc * P:(kc + 1) * P],
                                                  r[:, kc, hf * HALF:(hf + 1) * HALF], kc == 0 and p == 0, kc == KC - 1 and p == 2)
                    mm.then_inc(full, 1)

                def gate_up(c, i):
                    unit(gate_u(c), i, G[0], lambda: pe.wait_ge(gated, c + 2 * i), g_full)
                    unit(up_u(c), i, G[1], lambda: pe.wait_ge(hidden, c + 2 * i), u_full)

                def down(c, i):
                    b, u = c % 2, down_u(c)
                    pe.wait_ge(a_lo_done, c + 1 + 2 * i)
                    pe.wait_ge(W.lo_done, U0 + u + 1 + 6 * i)
                    for t in range(NT):
                        n = NT * c + t
                        if n >= 2:
                            pe.wait_ge(added, n - 1 + 2 * NT * i)
                        tok = slice(t * P, (t + 1) * P)
                        for p, (a, w) in enumerate(((a_lo, W.hi), (a_hi, W.lo), (a_hi, W.hi))):
                            for hf in range(2):
                                mm = weights_pass(pe, O[t % 2][:, hf * HALF:(hf + 1) * HALF], a[b][:, tok],
                                                  w[u % 2][:, hf * HALF:(hf + 1) * HALF], p == 0, p == 2)
                        mm.then_inc(o_full, 1)

                def chunk(c, i):
                    gate_up(c, i)
                    down(c - 1, i)

                in_order(pe, lambda: gate_up(0, 0), chunk, lambda: down(NCH - 1, 0))


PHASE_UNITS = dict(mixers1=3 + 3 * 10 + SECTIONS, merge=3 * 12, out1=KC, proj2=N_FEAT, out2=KC, ffn=3 * 22)
UNIT0 = {}
_n = 0
for _k, _v in PHASE_UNITS.items():
    UNIT0[_k] = _n
    _n += _v


def column_units(np, w, cols=P):
    k, n = w.shape
    return w.reshape(k // P, P, n // cols, cols).transpose(2, 1, 0, 3).reshape(n // cols, P, k // P * cols)


def layouts(np, I):
    L = {}
    w1 = column_units(np, I["w_in"][0])
    order = [24, 28, 32]
    for c in range(NC4):
        order += [4 * s + c for s in (9, 0, 1, 2, 4, 3, 5)]
        if c < NC4 - 1:
            order += [4 * s + c + 1 for s in (6, 7, 8)]
    parts = [w1[order]]
    for n in range(3):
        pb = column_units(np, I["w_branch"][0, n], 2 * P)
        for q in range(4):
            parts += [w1[40 + 8 * n + 2 * q:42 + 8 * n + 2 * q], pb[q:q + 1]]
    parts.append(I["w_out"][0].reshape(KC, P, D))
    w2 = I["w_in_2"][0]
    q, k, v, sz, xbc, dt, gqkv, gz, gb, ga = np.split(w2, [256, 384, 512, 1024, 2048, 2056, 2824, 3080, 3084], axis=1)
    q = q.reshape(D, 4, 64)[:, [0, 2, 1, 3]].reshape(D, 256)
    parts.append(column_units(np, np.concatenate([xbc, gqkv, sz, gz, q, k, v], axis=1)))
    parts.append(I["w_out_2"][0].reshape(KC, P, D))
    gate, up, down = column_units(np, I["ffn_w_gate_2"][0]), column_units(np, I["ffn_w_up_2"][0]), I["ffn_w_down_2"][0].reshape(22, P, D)
    parts += [gate[0:1], up[0:1]]
    for c in range(1, 22):
        parts += [gate[c:c + 1], up[c:c + 1], down[c - 1:c]]
    parts.append(down[21:])
    L["units"] = np.concatenate(parts)
    L["w_small"] = column_units(np, np.concatenate([dt, ga, gb], axis=1), SMALL)[0]

    chan = np.zeros((NC4, P, PAR), np.float32)
    chan[:, :, 0:3] = I["conv_w"][0].reshape(TAPS, NC4, P).transpose(1, 2, 0)
    chan[:, :, 3] = I["conv_b"][0].reshape(NC4, P)
    chan[:, :, 4] = I["pool_scale"][0].reshape(NC4, P)
    for c, w in enumerate(POOL_W):
        for n in range(4):
            chan[c, :, 5 + n] = float(2 ** n < w)
        chan[c, :, 9] = 1.0 / w
        chan[c, :, 10:] = 1.0 / np.minimum(np.arange(16) + 1, w)
    L["chan"] = chan
    L["pool_w"] = I["pool_w"][0]
    cp = np.zeros((P, CONV, 5), np.float32)
    cp[:, :8, 0:4] = I["ssd_conv_w_2"][0].reshape(4, 8, P).transpose(2, 1, 0)
    cp[:, :8, 4] = I["ssd_conv_b_2"][0].reshape(8, P).T
    cp[:, 8:, 0:4] = I["gdn_conv_w_2"][0].reshape(4, 6, P).transpose(2, 1, 0)
    L["conv_par"] = cp
    r = np.arange(P)
    before = r[:, None] < r[None, :]
    L["consts"] = np.stack([np.eye(P), before, -(r[:, None] >= r[None, :]).astype(float), -np.ones((P, P)),
                            r[:, None] <= r[None, :], np.ones((P, P))]).astype(np.float32)
    m = [np.where(r[:, None] <= r[None, :], 0.0, NEG)]
    for b in (1,) + LEVELS:
        lvl = (r[:, None] // (2 * b) == r[None, :] // (2 * b)) & (r[:, None] // b % 2 == 0) & (r[None, :] // b % 2 == 1)
        m.append(-lvl.astype(float) if b == 1 else lvl.astype(float))
    L["masks"] = np.stack(m).transpose(1, 0, 2).astype(np.float32)
    key = np.arange(256)
    dist = np.abs(r[:, None] + 128 - key[None, :]).astype(np.float64)
    chunk = key[None, :] // 64 - r[:, None] // 64
    valid = (chunk >= 0) & (chunk <= 2)
    slopes = 2.0 ** (-8.0 * np.arange(1, AH + 1) / AH)
    rest = np.stack([np.where(valid, -s * dist, NEG) for s in slopes], axis=1)
    first = np.where(key[None, None, :] >= 128, rest, NEG)
    L["attn_bias"] = np.stack([first, rest]).astype(np.float32)
    rows = [I["ssd_dt_bias_2"][0], I["gdn_dt_bias_2"][0], I["ssd_A_log_2"][0], I["gdn_A_log_2"][0], I["attn_sinks_2"][0],
            I["ssd_D_2"][0], I["ssd_norm_w_2"][0], I["gdn_norm_w_2"][0], np.array([64.0] * 4 + [1.0] * 4, np.float32)]
    L["rows"] = np.concatenate(rows).reshape(1, -1)
    for n in ("pre_norm_g", "post_norm_g", "pre_mix_norm_2", "post_mix_norm_2", "pre_ffn_norm_2", "post_ffn_norm_2"):
        L[n] = I[n]
    L["x"] = I["x"][0]
    return {k: np.ascontiguousarray(v) for k, v in L.items()}


CONSTS = ("ident", "before", "minus_from", "minus_one", "upto", "one")


def load_constants(nc, ctx, consts, W):
    C = {n: ctx.enter_context(nc.sbuf_tensor(f"c_{n}", [P, P], F32)) for n in CONSTS}
    here = ctx.enter_context(nc.semaphore("c_here"))
    with nc.Block() as block:
        @block.sync
        def _(sp):
            for i, n in enumerate(CONSTS):
                sp.dma_start(C[n][:], consts[i]).then_inc(here, 16)
            W.load(sp, 0)
            W.load(sp, 1)
            sp.wait_ge(here, 16 * len(CONSTS))
    return C


def load_rows(nc, ctx, src):
    rows = ctx.enter_context(nc.sbuf_tensor("par_rows", [P, ROW["end"]], F32))
    here = ctx.enter_context(nc.semaphore("rows_here"))
    with nc.Block() as block:
        @block.sync
        def _(sp):
            sp.dma_start(rows[:], src.to_broadcast([P, ROW["end"]])).then_inc(here, 16)
            sp.wait_ge(here, 16)
    return rows


def build(nc, A, out):
    dram = lambda n, s: nc.dram_tensor(n, s, F32, kind="Internal").ap()
    y_dram, feats = dram("y_branches", [3 * NC4, P, T]), dram("features2", [N_FEAT, P, T])
    x1, x2 = dram("x_layer1", [T, D]), dram("x_mixed", [T, D])

    def buffer(ctx, name, shape, dt=F32):
        return ctx.enter_context(nc.sbuf_tensor(name, shape, dt))

    def split_pair(ctx, name):
        return [buffer(ctx, f"{name}_{p}", [P, KC, T], F32R) for p in ("hi", "lo")]

    with ExitStack() as ctx:
        W = Stream(nc, ctx, A["units"])
        C = load_constants(nc, ctx, A["consts"], W)
        small = buffer(ctx, "small_cols", [P, NT, SMALL])
        feat_T = buffer(ctx, "features_T", [P, KC, T])
        with ExitStack() as s1:
            h = split_pair(s1, "h")
            first_norm(nc, C, A["x"], A["pre_norm_g"], *h)
            layer1_mixers(nc, C, W, *h, A["chan"], A["pool_w"], y_dram)
            layer1_merge(nc, W, UNIT0["merge"], *h, y_dram, feat_T)
            product_and_norms(nc, "o1", C, W, UNIT0["out1"], feat_T, A["x"], A["post_norm_g"], A["pre_mix_norm_2"], x1, *h)
            layer2_projections(nc, C, W, UNIT0["proj2"], *h, A["conv_par"], A["w_small"], feats, small)
        with ExitStack() as s2:
            rows = load_rows(nc, s2, A["rows"])
            prm = buffer(s2, "decay_par", [P, NT, PEND])
            layer2_decays(nc, C, small, rows, prm)
            layer2_mixers(nc, C, feats, rows, prm, A["masks"], A["attn_bias"], feat_T)
        with ExitStack() as s3:
            h = split_pair(s3, "h_ffn")
            product_and_norms(nc, "o2", C, W, UNIT0["out2"], feat_T, x1, A["post_mix_norm_2"], A["pre_ffn_norm_2"], x2, *h)
            layer2_ffn(nc, W, UNIT0["ffn"], *h, feat_T, x2, A["post_ffn_norm_2"], out)


def kernel(**inputs):
    import numpy as np
    import concourse.bacc as bacc
    from concourse.bass_utils import run_bass_kernel_spmd

    L = layouts(np, {k: np.asarray(v) for k, v in inputs.items()})
    nc = bacc.Bacc("TRN2", target_bir_lowering=False, num_devices=1)
    A = {k: nc.dram_tensor(f"in_{k}", v.shape, mybir.dt.from_np(v.dtype), kind="ExternalInput").ap() for k, v in L.items()}
    out = nc.dram_tensor("out", [T, D], F32, kind="ExternalOutput").ap()
    build(nc, A, out)
    r = run_bass_kernel_spmd(nc, [{f"in_{k}": v for k, v in L.items()}], core_ids=[0])
    return r.results[0]["out"].reshape(1, T, D)
```
